# Optimizing a Trainium2 kernel written in Bass

```python
import jax, jax.numpy as jnp
from jax import lax
import numpy as np

D_MODEL = 1024
BATCH = 1
SEQ = 512
DEPTH = 1

CHUNK = 64
D_SC = D_MODEL
SC_WIDTH = 3
D_CF = D_MODEL
CF_WIDTH = 31
D_POOL = D_MODEL
POOL_WINDOWS = (2, 4, 8, 16)
N_POOL_GROUPS = len(POOL_WINDOWS)
POOL_GROUP = D_POOL // N_POOL_GROUPS
N_BRANCHES = 3
SPLITS = np.cumsum([D_SC, D_SC, D_SC, D_CF, D_CF, D_POOL]).tolist()
IN_COLS = 3 * D_SC + 2 * D_CF + D_POOL + N_BRANCHES * D_MODEL
N_EXPERTS = 32
TOP_K = 4
D_FF = D_MODEL
SWIGLU_LIMIT = 7.0
SWIGLU_ALPHA = 1.702
EXPERT_BLOCK = 128
NORM_EPS = 1e-6
LN_EPS = 1e-5
N_MOD = 6

kernel_name = "hybrid_conv_pool_moe_streaming_block"

def rms_norm(x, g):
    x32 = x.astype(jnp.float32)
    y = x32 * lax.rsqrt(jnp.mean(x32 * x32, axis=-1, keepdims=True) + NORM_EPS)
    return (y * g.astype(jnp.float32)).astype(x.dtype)

def layer_norm(x, g, b):
    x32 = x.astype(jnp.float32)
    mu = jnp.mean(x32, axis=-1, keepdims=True)
    var = jnp.mean(jnp.square(x32 - mu), axis=-1, keepdims=True)
    y = (x32 - mu) * lax.rsqrt(var + LN_EPS)
    return (y * g.astype(jnp.float32) + b.astype(jnp.float32)).astype(x.dtype)

def causal_depthwise_conv(x, w):
    k = w.shape[0]
    return lax.conv_general_dilated(
        x, w[:, None, :].astype(x.dtype), window_strides=(1,), padding=[(k - 1, 0)],
        dimension_numbers=("NWC", "WIO", "NWC"), feature_group_count=x.shape[-1])

def multiscale_pool(u):
    t = u.shape[1]
    u32 = u.astype(jnp.float32)
    cs = jnp.cumsum(u32, axis=1)
    pos = jnp.arange(1, t + 1, dtype=jnp.float32)[None, :, None]
    outs = []
    for g, w in enumerate(POOL_WINDOWS):
        cg = cs[..., g * POOL_GROUP:(g + 1) * POOL_GROUP]
        lag = jnp.pad(cg[:, :t - w], ((0, 0), (w, 0), (0, 0)))
        outs.append((cg - lag) / jnp.minimum(pos, w))
    return (jnp.concatenate(outs, axis=-1) - u32).astype(u.dtype)

def mixer(h, w_in, sc_conv, sc_out, cf_conv, cf_conv_b, cf_ln_g, cf_ln_b, cf_out, cf_out_b,
          pool_w, pool_scale, w_o):
    bsz, t, d = h.shape
    proj = h @ w_in
    b_sc, c_sc, x_sc, a_cf, g_cf, u_pool, gate_logits = jnp.split(proj, SPLITS, axis=-1)
    y_a = (b_sc * causal_depthwise_conv(c_sc * x_sc, sc_conv)) @ sc_out
    v = a_cf * jax.nn.sigmoid(g_cf)
    v = causal_depthwise_conv(v, cf_conv) + cf_conv_b
    v = jax.nn.silu(layer_norm(v, cf_ln_g, cf_ln_b))
    y_b = v @ cf_out + cf_out_b
    p = multiscale_pool(u_pool).reshape(bsz, t, N_POOL_GROUPS, POOL_GROUP)
    y_c = jnp.einsum("btgi,gio->btgo", p, pool_w).reshape(bsz, t, d) * pool_scale
    gates = jax.nn.sigmoid(gate_logits).reshape(bsz, t, N_BRANCHES, d)
    merged = gates[:, :, 0] * y_a + gates[:, :, 1] * y_b + gates[:, :, 2] * y_c
    return merged @ w_o

def moe(h, w_router, b_router, w_gu, b_gu, w_down, b_down):
    bsz, t, d = h.shape
    n_tok = bsz * t
    ht = h.reshape(n_tok, d)
    logits = (ht @ w_router + b_router).astype(jnp.float32)
    top_val, top_idx = lax.top_k(logits, TOP_K)
    gate = jax.nn.softmax(top_val, axis=-1).astype(h.dtype)
    n_asg = n_tok * TOP_K
    flat_e = top_idx.reshape(n_asg).astype(jnp.int32)
    flat_tok = jnp.arange(n_asg, dtype=jnp.int32) // TOP_K
    flat_g = gate.reshape(n_asg)
    se, order = lax.sort_key_val(flat_e, jnp.arange(n_asg, dtype=jnp.int32))
    st = flat_tok[order]
    sg = flat_g[order]
    counts = jnp.bincount(flat_e, length=N_EXPERTS).astype(jnp.int32)
    padded = (counts + EXPERT_BLOCK - 1) // EXPERT_BLOCK * EXPERT_BLOCK
    ustart = jnp.cumsum(counts) - counts
    pend = jnp.cumsum(padded)
    pstart = pend - padded
    dest = pstart[se] + jnp.arange(n_asg, dtype=jnp.int32) - ustart[se]
    n_pad = n_asg + N_EXPERTS * EXPERT_BLOCK
    n_blocks = n_pad // EXPERT_BLOCK
    pad_tok = jnp.zeros((n_pad,), jnp.int32).at[dest].set(st)
    block_e = jnp.minimum(
        jnp.searchsorted(pend, jnp.arange(n_blocks, dtype=jnp.int32) * EXPERT_BLOCK, side="right"),
        N_EXPERTS - 1).astype(jnp.int32)
    xb = ht[pad_tok].reshape(n_blocks, EXPERT_BLOCK, d)

    def run_block(args):
        xblk, e = args
        hg = xblk @ w_gu[e] + b_gu[e]
        gt = jnp.minimum(hg[:, :D_FF], SWIGLU_LIMIT)
        up = jnp.clip(hg[:, D_FF:], -SWIGLU_LIMIT, SWIGLU_LIMIT)
        act = (up + 1.0) * gt * jax.nn.sigmoid(gt * SWIGLU_ALPHA)
        return act @ w_down[e] + b_down[e]

    yb = lax.map(run_block, (xb, block_e)).reshape(n_pad, d)
    y = jax.ops.segment_sum(yb[dest] * sg[:, None], st, num_segments=n_tok)
    return y.reshape(bsz, t, d)

def setup_inputs(seed: int = 0) -> dict:
    key = jax.random.key(seed)
    ks = jax.random.split(key, 32)
    f32 = jnp.float32
    d = D_MODEL

    def nrm(k, shape, scale):
        return jax.random.normal(k, shape, f32) * scale

    def gain(k, shape):
        return 1.0 + 0.05 * jax.random.normal(k, shape, f32)

    return {
        "x": nrm(ks[0], (BATCH, SEQ, d), 1.0),
        "c": nrm(ks[1], (BATCH, d), 1.0),
        "ada_w": nrm(ks[2], (DEPTH, d, N_MOD * d), 0.5 * d ** -0.5),
        "ada_b": nrm(ks[3], (DEPTH, N_MOD * d), 0.01),
        "mix_pre_g": gain(ks[4], (DEPTH, d)),
        "mix_post_g": gain(ks[5], (DEPTH, d)),
        "w_in": nrm(ks[6], (DEPTH, d, IN_COLS), d ** -0.5),
        "sc_conv": nrm(ks[7], (DEPTH, SC_WIDTH, D_SC), SC_WIDTH ** -0.5),
        "sc_out": nrm(ks[8], (DEPTH, D_SC, d), D_SC ** -0.5),
        "cf_conv": nrm(ks[9], (DEPTH, CF_WIDTH, D_CF), CF_WIDTH ** -0.5),
        "cf_conv_b": nrm(ks[10], (DEPTH, D_CF), 0.01),
        "cf_ln_g": gain(ks[11], (DEPTH, D_CF)),
        "cf_ln_b": nrm(ks[12], (DEPTH, D_CF), 0.01),
        "cf_out": nrm(ks[13], (DEPTH, D_CF, d), D_CF ** -0.5),
        "cf_out_b": nrm(ks[14], (DEPTH, d), 0.01),
        "pool_w": nrm(ks[15], (DEPTH, N_POOL_GROUPS, POOL_GROUP, POOL_GROUP), POOL_GROUP ** -0.5),
        "pool_scale": gain(ks[16], (DEPTH, d)),
        "w_o": nrm(ks[17], (DEPTH, d, d), d ** -0.5),
        "moe_pre_g": gain(ks[18], (DEPTH, d)),
        "moe_post_g": gain(ks[19], (DEPTH, d)),
        "w_router": nrm(ks[20], (DEPTH, d, N_EXPERTS), d ** -0.5),
        "b_router": nrm(ks[21], (DEPTH, N_EXPERTS), 0.01),
        "w_gu": nrm(ks[22], (DEPTH, N_EXPERTS, d, 2 * D_FF), d ** -0.5),
        "b_gu": nrm(ks[23], (DEPTH, N_EXPERTS, 2 * D_FF), 0.01),
        "w_down": nrm(ks[24], (DEPTH, N_EXPERTS, D_FF, d), D_FF ** -0.5),
        "b_down": nrm(ks[25], (DEPTH, N_EXPERTS, d), 0.01),
    }

def reference(x, c, ada_w, ada_b, mix_pre_g, mix_post_g, w_in, sc_conv, sc_out, cf_conv, cf_conv_b,
              cf_ln_g, cf_ln_b, cf_out, cf_out_b, pool_w, pool_scale, w_o, moe_pre_g, moe_post_g,
              w_router, b_router, w_gu, b_gu, w_down, b_down):
    bsz, _, d = x.shape
    c_act = jax.nn.silu(c)
    for l in range(DEPTH):
        mod = (c_act @ ada_w[l] + ada_b[l]).reshape(bsz, N_MOD, 1, d)
        shift1, scale1, gate1, shift2, scale2, gate2 = (mod[:, i] for i in range(N_MOD))
        h = rms_norm(x, mix_pre_g[l]) * (1.0 + scale1) + shift1
        y = mixer(h, w_in[l], sc_conv[l], sc_out[l], cf_conv[l], cf_conv_b[l], cf_ln_g[l], cf_ln_b[l],
                  cf_out[l], cf_out_b[l], pool_w[l], pool_scale[l], w_o[l])
        x = x + gate1 * rms_norm(y, mix_post_g[l])
        h = rms_norm(x, moe_pre_g[l]) * (1.0 + scale2) + shift2
        y = moe(h, w_router[l], b_router[l], w_gu[l], b_gu[l], w_down[l], b_down[l])
        x = x + gate2 * rms_norm(y, moe_post_g[l])
    return x


_drawn_inputs = setup_inputs


def setup_inputs(seed=0):
    import zlib

    import numpy as np

    out = dict(_drawn_inputs(seed))
    spreads = {}
    factors = {'cf_conv_b': 6.347,
     'cf_ln_g': 4.029,
     'cf_ln_b': 8.0,
     'cf_out_b': 8.0,
     'pool_scale': 2.89,
     'moe_post_g': 3.995,
     'b_router': 3.721,
     'b_gu': 8.0,
     'b_down': 8.0}
    for name, (base, spread) in spreads.items():
        noise = np.random.default_rng([zlib.crc32(name.encode()), seed]).standard_normal(out[name].shape)
        drawn = base * np.exp(spread * noise) if base else spread * noise
        out[name] = __import__('jax').numpy.asarray(drawn.astype(out[name].dtype))
    for name, factor in factors.items():
        out[name] = (out[name] * factor).astype(out[name].dtype)
    return out
```

```python
from contextlib import ExitStack

import concourse.bass as bass
from concourse import mybir

ALU = mybir.AluOpType
ACT = mybir.ActivationFunctionType
AX = mybir.AxisListType
F32 = mybir.dt.float32
F32R = mybir.dt.float32r
I32 = mybir.dt.int32
U32 = mybir.dt.uint32
ds = bass.ds

P = 128
D = 1024
T = 512
KC = D // P
TT = T // P
HALF = 512
EXPERTS = 32
TOP_K = 4
NORM_EPS = 1e-6
LN_EPS = 1e-5
LIMIT = 7.0
ALPHA = 1.702
SC_W = 3
CF_W = 31
CF_PAD = CF_W - 1
POOLS = 4
MAX_WIN = 16
SUM_PAD = 32

R_C, R_MIXG, R_SHIFT1, R_SCALE1, R_CFB, R_LNG, R_LNB, R_CFOB, R_POOLS, R_SC = 0, 1, 2, 3, 4, 5, 6, 7, 8, 9
R_CF = R_SC + SC_W
N_ROWS = R_CF + CF_W

RING = 4
N_A, N_B, N_C, N_D, N_E, N_G, N_F = 0, 16, 48, 64, 80, 88, 96
TAPS = {"A": (0, 9), "B": (9, 19), "C": (19, 28), "D": (28, CF_W)}

CH = 24
RAW_RING = 12
SPLIT_RING = 10
WHOLE = (7, 15, 19, 23)
SPLITS = [c for c in range(CH) if c not in WHOLE]
NS = len(SPLITS)
AHEAD = 4
P_CHAIN0, P_AE0, P_CHAIN1, P_AE1 = 12, 14, 20, 22


def splits_before(c):
    return sum(s < c for s in SPLITS)

MAX_OVER = T * TOP_K // P - 1
NO_ROW = 4 * T * TOP_K


def build(nc, x, cond, ada_w, ada_b, mix_pre_g, mix_post_g, w_in, sc_conv, sc_out, cf_conv, cf_conv_b,
          cf_ln_g, cf_ln_b, cf_out, cf_out_b, pool_w, pool_scale, w_o, moe_pre_g, moe_post_g,
          w_router, b_router, w_gu, b_gu, w_down, b_down, out):
    with ExitStack() as ctx:
        KB = 1024
        base = (nc.sbuf_base + 63) // 64 * 64

        def at(name, off, shape, dt=F32):
            return nc.alloc_sbuf_tensor_at(name, shape, dt, offset=base + off)

        def sem(name):
            return ctx.enter_context(nc.semaphore(name))

        o_merged, o_rows, o_v, o_p, o_cv, o_ht, o_s, o_raw, o_split, o_misc = (
            0, 16 * KB, 32 * KB, 49 * KB, 65 * KB, 81 * KB, 113 * KB, 145 * KB, 161 * KB, 193 * KB)
        x_in = at("x_in", o_rows, [P, TT, D])
        prow = at("prow", o_merged, [P, D])
        xT = at("xT", o_p, [P, KC, T])
        ada1 = at("ada1", o_ht, [P, KC, 2 * D])
        hT = at("hT", o_ht, [P, 2, KC, T], F32R)
        htmp = at("htmp", o_merged, [P, KC, T])
        v = at("v", o_v, [P, KC, CF_PAD + T])
        cv = at("cv", o_cv, [P, KC, T])
        sT = at("sT", o_s, [P, 2, KC, T], F32R)
        pT = at("pT", o_p, [P, KC, T])
        c_sb = at("c_sb", o_merged + 4 * KB, [P, T])
        cxp = at("cxp", o_merged + 6 * KB, [P, SC_W - 1 + T])
        t3 = at("t3", o_merged + 9 * KB, [P, T])
        csp = at("csp", o_merged + 11 * KB + 256, [P, SUM_PAD + T])
        merged = at("merged", o_merged, [P, KC, T])
        pS = at("pS", o_s, [P, 2, 2, T], F32R)
        acc1 = at("acc1", o_cv, [P, 2 * D])
        sgp = at("sgp", o_p + KB, [P, KC - 1, T])
        mu = at("mu", o_v, [P, T])
        lrs = at("lrs", o_v + 2 * KB, [P, T])
        sq = at("sq", o_v + 4 * KB, [P, 2, T])
        zl = at("zl", o_v + 8 * KB, [P, 2, T])
        vT = at("vT", o_s, [P, 2, KC, T], F32R)
        mT = at("mT", o_v, [P, 2, KC, T], F32R)
        ada_ring = at("ada_ring", o_cv, [P, RING, D])
        rows = at("rows", o_rows, [P, 4, D])
        raw = at("raw", o_raw, [P, RING, D])
        split = at("split", o_split, [P, RING, 2, D], F32R)
        pcol = at("pcol", o_misc, [P, KC, N_ROWS])
        o = o_misc + 1408
        ident = at("ident", o, [P, P]); o += 512
        mean_w = at("mean_w", o, [P, P]); o += 512
        ones = at("ones", o, [P, P]); o += 512
        sg = at("sg", o, [P, 2, T]); o += 4 * KB
        tmp = at("tmp", o, [P, 2, T]); o += 4 * KB
        corr = at("corr", o, [P, KC, MAX_WIN]); o += 512
        invw = at("invw", o, [P, KC]); o += 32
        pos = at("pos", o, [P, MAX_WIN]); o += 64
        pos_i = at("pos_i", o, [P, MAX_WIN], I32); o += 64
        xtra = at("xtra", o, [P, T]); o += 2 * KB
        cact = at("cact", o, [P, KC]); o += 32
        csig = at("csig", o, [P, KC]); o += 32
        mod1 = at("mod1", o, [P, 2, KC]); o += 64
        ss = at("ss", o, [P, TT]); o += 32
        rs = at("rs", o, [P, TT]); o += 32
        rr = at("rr", o, [P, TT]); o += 32

        ps = ctx.enter_context(nc.psum_tensor("ps", [P, 8, HALF], F32))

        o_2 = o_v
        x2 = at("x2", o_merged, [P, TT, D])
        bias = at("bias", o_rows, [2 * EXPERTS, 3 * D], F32R)
        h2 = at("h2", o_2, [P, TT, D])
        scrap = at("scrap", o_2 + 16 * KB, [P, D])
        ynorm = at("ynorm", o_2 + 20 * KB, [P, D])
        h2T = at("h2T", o_2 + 24 * KB, [P, 2, KC, P])
        brow0 = at("brow0", o_misc + 1408 + 1536 + 4 * KB, [1, D])
        brow = at("brow", o_s, [1, 3, D])
        gbc = at("gbc", o_s + 12 * KB, [P, 3, D])
        bst = at("bst", o_s + 64 * KB, [2 * EXPERTS, 3 * D])
        xg = at("xg", o_2, [P, D])
        yg = at("yg", o_2 + 4 * KB, [P, D])
        xe = at("xe", o_2 + 8 * KB, [P, 2, KC, P], F32R)
        ae = at("ae", o_2 + 16 * KB, [P, 2, KC, P], F32R)
        craw2 = [at(f"craw2_{p}", (o_ht + p * 8 * KB) if p < 4 else o_cv + (p - 4) * 8 * KB, [P, 2, D]) for p in range(RAW_RING // 2)]
        craw = [craw2[s // 2][:, s % 2, :] for s in range(RAW_RING)]
        csplit = at("csplit", o_s, [P, SPLIT_RING, 2, D], F32R)
        scrap2 = at("scrap2", o_2, [P, D])
        yt = at("yt", o_ht, [P, TT, TOP_K, D])
        o = o_2 + 24 * KB
        gt = at("gt", o, [P, HALF]); o += 2 * KB
        sgm = at("sgm", o, [P, HALF]); o += 2 * KB
        ua = at("ua", o, [P, HALF]); o += 2 * KB
        xe_w = at("xe_w", o, [P, P]); o += 512
        ae_w = at("ae_w", o, [P, 2, P]); o += 1024
        o = o_misc + 1408 + 1536
        wr = at("wr", o, [P, KC, EXPERTS]); o += KB
        brt = at("brt", o, [P, EXPERTS]); o += 128
        iota_e = at("iota_e", o, [P, P]); o += 512
        tri = at("tri", o, [P, P]); o += 512
        eye2 = at("eye2", o, [2 * EXPERTS, EXPERTS]); o += 128
        pidx_i = at("pidx_i", o, [P, 1], I32); o += 32
        pidx = at("pidx", o, [P, 1]); o += 32
        logits = at("logits", o, [P, TT, EXPERTS]); o += 512
        assert o <= o_misc + 1408 + 1536 + 4 * KB
        o = o_misc + 1408 + 1536 + 4 * KB
        top = at("top", o, [P, TT, 8]); o += 128
        topi = at("topi", o, [P, TT, 8], U32); o += 128
        negmax = at("negmax", o, [P, TT]); o += 32
        ex = at("ex", o, [P, TT, TOP_K]); o += 64
        exsum = at("exsum", o, [P, TT]); o += 32
        exinv = at("exinv", o, [P, TT]); o += 32
        idxf = at("idxf", o, [P, TT, TOP_K]); o += 64
        rank = at("rank", o, [P, TT, TOP_K]); o += 64
        beyond = at("beyond", o, [P, TT, TOP_K]); o += 64
        place_f = at("place_f", o, [P, TT, TOP_K]); o += 64
        place = at("place", o, [P, TT * TOP_K], I32); o += 64
        mark = at("mark", o, [P, TT, EXPERTS]); o += 512
        flags = at("flags", o, [P, EXPERTS, 4]); o += 512
        prefix = at("prefix", o, [P, P]); o += 512
        chosen = at("chosen", o, [P, P]); o += 512
        code = at("code", o, [P, 1]); o += 32
        code_row = at("code_row", o, [1, 16], I32); o += 64
        n_over_i = at("n_over_i", o, [1, 1], I32); o += 32
        iota_i = at("iota_i", o, [P, P], I32)
        token_of = at("token_of", o, [P, P], I32); o += 512
        st2 = at("st2", o, [P, 6, TT]); o += 96
        assert o <= o_misc + 1408 + 1536 + 8 * KB, o - o_misc
        o = o_misc
        hot = at("hot", o, [2 * EXPERTS, P], F32R); o += 512
        tok_now = at("tok_now", o, [P, 1], I32); o += 32
        asg_now = at("asg_now", o, [P, 1], I32); o += 32
        gate_now = at("gate_now", o, [P, 1]); o += 32
        fence = at("fence", o, [P, 3]); o += 32
        pay = at("pay", o, [P, TT * TOP_K, 2], I32); o += 128
        assert o <= o_misc + 1408
        onehots = at("onehots", o_2 + 16 * KB, [P, TT, TOP_K, EXPERTS])
        picked = at("picked", o_2 + 18 * KB, [P, TT, TOP_K, EXPERTS])
        table = at("table", o_misc + 14080, [P, P, 2], I32)
        h2_rows = nc.dram_tensor("h2_rows", (T, D), F32).ap()
        y_rows = nc.dram_tensor("y_rows", (T * TOP_K, D), F32).ap()
        table_d = nc.dram_tensor("table_d", (P * P, 2), I32).ap()

        prow_full, x_full, consts = sem("prow_full"), sem("x_full"), sem("consts")
        ada1_full = [sem(f"ada1_full{i}") for i in range(KC)]
        acc1_step = sem("acc1_step")
        pcol_mm, pcol_done, sig_c, cact_done = sem("pcol_mm"), sem("pcol_done"), sem("sig_c"), sem("cact_done")
        ss_done, ms_done, sq_done, rs_done, xn_done = sem("ss_done"), sem("ms_done"), sem("sq_done"), sem("rs_done"), sem("xn_done")
        xT_mm, xT_done, mod_mm, mod_step = sem("xT_mm"), sem("xT_done"), sem("mod_mm"), sem("mod_step")
        h_f, h_hi, h_lo = sem("h_f"), sem("h_hi"), sem("h_lo")
        raw_full = [sem(f"raw_full{i}") for i in range(RING)]
        w_hi, w_lo = sem("w_hi"), sem("w_lo")
        mm_done = sem("mm_done")
        bank_read = sem("bank_read")
        sg_done, conv, g1_done = sem("sg_done"), sem("conv"), sem("g1_done")
        c_done, cx_done, t3_step, s_f, s_hi, s_lo = sem("c_done"), sem("cx_done"), sem("t3_step"), sem("s_f"), sem("s_hi"), sem("s_lo")
        pool_step = sem("pool_step")
        p_hi, p_lo, mg_step = sem("p_hi"), sem("p_lo"), sem("mg_step")
        mean_mm, mu_done, cen_done, sq2_done, var_mm, var_e, lsd_done, lrs_done = (
            sem("mean_mm"), sem("mu_done"), sem("cen_done"), sem("sq2_done"), sem("var_mm"), sem("var_e"), sem("lsd_done"), sem("lrs_done"))
        xh_done, z_done, vf_done, v_hi, v_lo = sem("xh_done"), sem("z_done"), sem("vf_done"), sem("v_hi"), sem("v_lo")
        m_hi, m_lo = sem("m_hi"), sem("m_lo")
        ada_full = [sem(f"ada_full{i}") for i in range(RING)]
        ada_used = sem("ada_used")
        row_mm, row_done = sem("row_mm"), sem("row_done")
        brow0_full, brow_full, gbc_full, x2_full, wr_full = (
            sem("brow0_full"), sem("brow_full"), sem("gbc_full"), sem("x2_full"), sem("wr_full"))
        g1_ready, sqy_done, x2_step, x2_done, sqx_done = sem("g1_ready"), sem("sqy_done"), sem("x2_step"), sem("x2_done"), sem("sqx_done")
        stat, sd_done, mod2_done, b2_done, h2_step, h2_done = (
            sem("stat"), sem("sd_done"), sem("mod2_done"), sem("b2_done"), sem("h2_step"), sem("h2_done"))
        h2_tr, h2T_done, logit_mm, h2_stored = sem("h2_tr"), sem("h2T_done"), sem("logit_mm"), sem("h2_stored")
        routed, negmax_done, exp_done = sem("routed"), sem("negmax_done"), sem("exp_done")
        mark_done, rank_mm, code_done, code_mm, codes_ready = (
            sem("mark_done"), sem("rank_mm"), sem("code_done"), sem("code_mm"), sem("codes_ready"))
        consts2, place_ready, gates_ready = sem("consts2"), sem("place_ready"), sem("gates_ready")
        table_set, table_cleared, table_put, table_full, tokens_ready = (
            sem("table_set"), sem("table_cleared"), sem("table_put"), sem("table_full"), sem("tokens_ready"))
        bst_full, bias_hi, bias_ready = sem("bst_full"), sem("bias_hi"), sem("bias_ready")
        craw_full = [sem(f"craw_full{p}") for p in range(RAW_RING // 2)]
        c_hi = sem("c_hi")
        c_lo = sem("c_lo")
        c_mm = sem("c_mm")
        xg_full, xe_tr, xe_hi, xe_lo = sem("xg_full"), sem("xe_tr"), sem("xe_hi"), sem("xe_lo")
        hot_ready, hot_used, gate_ready, asg_ready = sem("hot_ready"), sem("hot_used"), sem("gate_ready"), sem("asg_ready")
        tok_ready = sem("tok_ready")
        gt_done, clip_done, up_done, act_done, sgm_done = (
            sem("gt_done"), sem("clip_done"), sem("up_done"), sem("act_done"), sem("sgm_done"))
        ae_tr, ae_hi, ae_lo, yg_done, y_put = sem("ae_tr"), sem("ae_hi"), sem("ae_lo"), sem("yg_done"), sem("y_put")
        moe_done = sem("moe_done")
        yt_full = [sem(f"yt_full{t}") for t in range(TT)]
        sum_step, sqz_done, stat3, sd3_done, out_step, out_ready, stored = (
            sem("sum_step"), sem("sqz_done"), sem("stat3"), sem("sd3_done"), sem("out_step"), sem("out_ready"), sem("stored"))

        def w_in_block(col, i):
            return w_in[0, :, ds(i * P + col, P)].rearrange("(k p) n -> p k n", p=P)

        def square_block(w, i):
            return w[0, :, ds(i * P, P)].rearrange("(k p) n -> p k n", p=P)

        raw_blk = [raw[:, s, :].rearrange("p (k n) -> p k n", k=KC) for s in range(RING)]

        block = ctx.enter_context(nc.Block())

        @block.sync
        def _(sp):
            sp.dma_start(x_in[:], x[0].rearrange("(t p) n -> p t n", p=P)).then_inc(x_full, 16)
            for r, src in ((R_C, cond), (R_MIXG, mix_pre_g), (R_CFB, cf_conv_b), (R_LNG, cf_ln_g), (R_LNB, cf_ln_b),
                           (R_CFOB, cf_out_b), (R_POOLS, pool_scale)):
                sp.dma_start(prow[r:r + 1, :], src[0:1, :]).then_inc(prow_full, 16)
            sp.dma_start(prow[R_SHIFT1:R_SHIFT1 + 2, :], ada_b[0, 0:2 * D].rearrange("(r n) -> r n", r=2)).then_inc(prow_full, 16)
            sp.dma_start(prow[R_SC:R_SC + SC_W, :], sc_conv[0]).then_inc(prow_full, 16)
            sp.dma_start(prow[R_CF:R_CF + CF_W, :], cf_conv[0]).then_inc(prow_full, 16)
            for k in range(KC):
                sp.dma_start(ada1[:, k, :], ada_w[0, k * P:(k + 1) * P, 0:2 * D]).then_inc(ada1_full[k], 16)

            def load(n, s, dst, src):
                if not isinstance(src.offset, int):
                    sp.lower_val(src.offset * 4)
                sp.wait_ge(w_lo, n + 1)
                sp.dma_start(dst, src).then_inc(raw_full[s], 16)

            def chunk_pair(e, c):
                k = c % 8
                if c < 16:
                    h = c // 8
                    return w_gu[0, ds(e, 1), k * P:(k + 2) * P, :].rearrange("e (p i) (u n) -> p (e i u) n", i=2, u=2)[:, :, h * HALF:(h + 1) * HALF]
                return w_down[0, ds(e, 1), k * P:(k + 2) * P, :].rearrange("e (p i) n -> p (e i n)", i=2)

            def pair_slots(c):
                dst = craw2[c // 2 % (RAW_RING // 2)]
                return dst[:, :, :].rearrange("p k (u n) -> p (k u) n", u=2) if c < 16 else dst[:, :, :].rearrange("p k n -> p (k n)")

            def first_pair(c):
                sp.dma_start(pair_slots(c), chunk_pair(0, c)).then_inc(craw_full[c // 2], 16)

            def next_pair(blk, e, c):
                src = chunk_pair(e, c)
                if not isinstance(src.offset, int):
                    sp.lower_val(src.offset * 4)
                last = (c + 1 - RAW_RING) % CH
                of = blk + 1 if c >= RAW_RING else blk
                if last in WHOLE:
                    sp.wait_ge(c_mm, of * CH + (last + 1))
                else:
                    sp.wait_ge(c_lo, of * NS + splits_before(last + 1))
                sp.dma_start(pair_slots(c), src).then_inc(craw_full[c // 2 % (RAW_RING // 2)], 16)

            with sp.Fori(0, 4) as j:
                for s in range(RING):
                    load(j * 4 + (N_A + s), s, raw_blk[s], w_in_block((3 + s % 2) * D, j * 2 + s // 2))
            with sp.Fori(0, 8) as i:
                for s, part in enumerate((1, 2, 0, 5)):
                    load(i * 4 + (N_B + s), s, raw_blk[s], w_in_block(part * D, i))
            with sp.Fori(0, 4) as j:
                for s in range(RING):
                    i = j * 2 + s // 2
                    load(j * 4 + (N_C + s), s, raw_blk[s], w_in_block(6 * D, i) if s % 2 == 0 else square_block(sc_out, i))
            for g in range(POOLS):
                for s in range(RING):
                    h = s // 2
                    if s % 2 == 0:
                        load(N_D + 4 * g + s, s, raw_blk[s], w_in_block(8 * D, 2 * g + h))
                    else:
                        load(N_D + 4 * g + s, s, raw_blk[s][:, 0:2, :],
                             pool_w[0, g, :, h * P:(h + 1) * P].rearrange("(k p) n -> p k n", p=P))
            with sp.Fori(0, 2) as j:
                for s in range(RING):
                    load(j * 4 + (N_E + s), s, raw_blk[s], w_in_block(7 * D, j * 4 + s))
            with sp.Fori(0, 2) as j:
                for s in range(RING):
                    load(j * 4 + (N_G + s), s, raw_blk[s], square_block(cf_out, j * 4 + s))
            sp.wait_ge(vf_done, KC)
            sp.dma_start(brow0[0:1, :], ada_b[0:1, 2 * D:3 * D]).then_inc(brow0_full, 16)
            sp.wait_ge(mm_done, N_G + RING)
            for c in range(0, 8, 2):
                first_pair(c)
            for k in range(KC):
                load(N_F + k, k % RING, raw[:, k % RING, :], w_o[0, k * P:(k + 1) * P, :])
            sp.wait_ge(mm_done, N_F + RING)
            sp.dma_start(brow[0:1, :, :], ada_b[0:1, 3 * D:6 * D].rearrange("a (r n) -> a r n", r=3)).then_inc(brow_full, 16)
            for r, src in enumerate((mix_post_g, moe_pre_g, moe_post_g)):
                sp.dma_start(gbc[:, r, :], src[0:1, :].broadcast_to((P, D))).then_inc(gbc_full, 16)
            sp.wait_ge(m_lo, KC)
            sp.dma_start(x2[:], x[0].rearrange("(t p) n -> p t n", p=P)).then_inc(x2_full, 16)
            sp.dma_start(wr[:, :, :], w_router[0].rearrange("(k p) e -> p k e", p=P)).then_inc(wr_full, 16)
            sp.dma_start(brt[:, :], b_router[0:1, :].broadcast_to((P, EXPERTS))).then_inc(wr_full, 16)
            sp.wait_ge(ada_used, 4 * KC + RING)
            for c in range(8, RAW_RING, 2):
                first_pair(c)
            sp.wait_ge(mm_done, N_F + KC + RING)
            for a in range(2):
                rows_a = slice(a * EXPERTS, (a + 1) * EXPERTS)
                sp.dma_start(bst[rows_a, 0:2 * D], b_gu[0]).then_inc(bst_full, 16)
                sp.dma_start(bst[rows_a, 2 * D:3 * D], b_down[0]).then_inc(bst_full, 16)
            for t in range(TT):
                sp.wait_ge(h2_done, t + 1)
                sp.dma_start(h2_rows[t * P:(t + 1) * P, :], h2[:, t, :]).then_inc(h2_stored, 16)

            with sp.Fori(0, EXPERTS - 1) as j:
                for c in range(RAW_RING, CH, 2):
                    next_pair(j, j, c)
                for c in range(0, RAW_RING, 2):
                    next_pair(j + 1, j + 1, c)
            for c in range(RAW_RING, CH, 2):
                next_pair(EXPERTS - 1, EXPERTS - 1, c)
            sp.wait_ge(codes_ready, 2)
            n_over = sp.value_load(n_over_i[0:1, 0:1], min_val=0, max_val=MAX_OVER)
            with sp.Fori(0, MAX_OVER) as j:
                with sp.If(j < n_over):
                    code_j = sp.value_load(code_row[0:1, ds(j, 1)], min_val=0, max_val=P - 1)
                    for c in range(0, CH, 2):
                        next_pair(j + EXPERTS, code_j // 4, c)
            sp.wait_ge(moe_done, 1)
            for t in range(TT):
                sp.dma_start(yt[:, t, :, :], y_rows[t * P * TOP_K:(t + 1) * P * TOP_K, :].rearrange("(p k) n -> p k n", k=TOP_K)).then_inc(yt_full[t], 16)
            for t in range(TT):
                sp.wait_ge(out_ready, t + 1)
                sp.dma_start(out[0, t * P:(t + 1) * P, :], x2[:, t, :]).then_inc(stored, 16)
            sp.wait_ge(stored, TT * 16)

        @block.scalar
        def _(act):
            act.wait_ge(x_full, 16)
            for t in range(TT):
                act.activation(tmp[:, :, :].rearrange("p a b -> p (a b)"), x_in[:, t, :], ACT.Square,
                               accum_out=ss[:, t:t + 1]).then_inc(ss_done, 1)
                act.wait_ge(ss_done, t + 1)
            act.wait_ge(ms_done, 1)
            act.activation(rr[:, :], rs[:, :], ACT.Sqrt).then_inc(sq_done, 1)
            act.wait_ge(pcol_mm, 1)
            act.activation(pcol[:, :, :], ps[:, 0, 0:KC * N_ROWS].rearrange("p (k r) -> p k r", k=KC), ACT.Copy).then_inc(pcol_done, 1)
            act.wait_ge(pcol_done, 1)
            act.activation(csig[:, :], pcol[:, :, R_C], ACT.Sigmoid).then_inc(sig_c, 1)
            for k in range(KC):
                act.wait_ge(xT_mm, k + 1)
                act.activation(xT[:, k, :], ps[:, 1 + k % 4, :], ACT.Copy).then_inc(xT_done, 1)

            def hi(n, s, cols=D):
                act.wait_ge(raw_full[s], (n // RING) * 16 + 16)
                act.wait_ge(mm_done, n + 1)
                act.activation(split[:, s, 0, 0:cols], raw[:, s, 0:cols], ACT.Copy).then_inc(w_hi, 1)

            def hi_at(j, n0, s, cols=D):
                act.wait_ge(raw_full[s], j * 16 + (n0 // RING * 16 + 16))
                act.wait_ge(mm_done, j * 4 + (n0 + 1))
                act.activation(split[:, s, 0, 0:cols], raw[:, s, 0:cols], ACT.Copy).then_inc(w_hi, 1)

            def sigmoid(b, par, n):
                act.wait_ge(bank_read, n + 2)
                act.activation(sg[:, par, :], ps[:, b, :], ACT.Sigmoid).then_inc(sg_done, 1)

            hi(0, 0)
            hi(1, 1)
            for k in range(KC):
                act.wait_ge(h_f, k + 1)
                act.activation(hT[:, 0, k, :], htmp[:, k, :], ACT.Copy).then_inc(h_hi, 1)
            with act.Fori(0, 4) as j:
                for q in range(2):
                    n = N_A + 2 * q
                    hi_at(j, n + 2, (n + 2) % RING)
                    hi_at(j, n + 3, (n + 3) % RING)
                    act.wait_ge(mm_done, j * 4 + (n + 2 + RING))
                    sigmoid(2 * q + 1, q, j * 4 + n)
            with act.Fori(0, 8) as i:
                n = N_B
                hi_at(i, n + 2, 2)
                hi_at(i, n + 3, 3)
                act.wait_ge(mm_done, i * 4 + (n + 1 + RING))
                act.wait_ge(bank_read, i * 4 + (n + RING))
                act.activation(c_sb[:, :], ps[:, 0, :], ACT.Copy).then_inc(c_done, 1)
                hi_at(i, n + 4, 0)
                hi_at(i, n + 5, 1)
                act.wait_ge(s_f, i + 1)
                act.activation(sT[:, 0, ds(i, 1), :].rearrange("p a n -> p (a n)"), t3[:, :], ACT.Copy).then_inc(s_hi, 1)
            with act.Fori(0, 4) as j:
                for q in range(2):
                    n = N_C + 2 * q
                    hi_at(j, n + 2, (n + 2) % RING)
                    hi_at(j, n + 3, (n + 3) % RING)
                    act.wait_ge(mm_done, j * 4 + (n + 1 + RING))
                    sigmoid(2 * q, q, j * 4 + n)
            for g in range(POOLS):
                n = N_D + 4 * g
                act.wait_ge(mm_done, n + RING)
                for h in range(2):
                    act.activation(pS[:, 0, h, :], pT[:, 2 * g + h, :], ACT.Copy).then_inc(p_hi, 1)
                hi(n + 2, 2)
                hi(n + 3, 3, 2 * P)
                for h in range(2):
                    act.wait_ge(mm_done, n + 2 * h + 1 + RING)
                    sigmoid(2 * h, h, n + 2 * h)
                    if h == 0:
                        hi(n + 4, 0)
                        hi(n + 5, 1, 2 * P if g < POOLS - 1 else D)

            def gate1(i):
                act.wait_ge(mm_done, N_E + i + 1 + RING)
                act.wait_ge(p_lo, KC)
                act.wait_ge(sg_done, 3 * KC)
                gate = sgp[:, i, :] if i < KC - 1 else sg[:, 0, :]
                act.activation(gate, ps[:, i % RING, :], ACT.Sigmoid).then_inc(g1_done, 1)

            def square(k):
                act.wait_ge(cen_done, k + 1)
                if k >= 2:
                    act.wait_ge(var_mm, k - 1)
                act.activation(sq[:, k % 2, :], cv[:, k, :], ACT.Square).then_inc(sq2_done, 1)

            def norm(k):
                act.wait_ge(xh_done, k + 1)
                if k >= 2:
                    act.wait_ge(vf_done, k - 1)
                act.activation(tmp[:, k % 2, :], cv[:, k, :], ACT.Sigmoid, bias=pcol[:, k, R_LNB:R_LNB + 1],
                               scale=pcol[:, k, R_LNG:R_LNG + 1]).then_inc(z_done, 1)
                act.activation(zl[:, k % 2, :], cv[:, k, :], ACT.Identity, bias=pcol[:, k, R_LNB:R_LNB + 1],
                               scale=pcol[:, k, R_LNG:R_LNG + 1]).then_inc(z_done, 1)

            def norm_hi(k):
                act.wait_ge(vf_done, k + 1)
                act.activation(vT[:, 0, k, :], cv[:, k, :], ACT.Copy).then_inc(v_hi, 1)

            for i in range(KC):
                hi(N_E + i + 2, (i + 2) % RING)
                if i == 1:
                    act.wait_ge(mean_mm, 1)
                    act.activation(mu[:, :], ps[:, 4, :], ACT.Copy).then_inc(mu_done, 1)
                gate1(i)
                if i in (1, 2):
                    for k in range(4 * (i - 1), 4 * i):
                        square(k)
                if i == 3:
                    act.wait_ge(var_e, 1)
                    act.activation(lrs[:, :], lrs[:, :], ACT.Sqrt).then_inc(lsd_done, 1)
                if i >= 4:
                    for k in range(2 * (i - 4), 2 * (i - 4) + 2):
                        norm(k)
                        if k >= 1:
                            norm_hi(k - 1)
            norm_hi(KC - 1)
            for i in range(KC):
                hi(N_G + i + 2, (i + 2) % RING)
                act.wait_ge(mg_step, KC + i + 1)
                act.activation(mT[:, 0, i, :], merged[:, i, :], ACT.Copy).then_inc(m_hi, 1)
            for h in range(2):
                act.wait_ge(row_mm, h + 1)
                act.activation(rows[:, 0, h * HALF:(h + 1) * HALF], ps[:, 4 + h, :], ACT.Copy).then_inc(row_done, 1)
            for k in range(2, KC):
                hi(N_F + k, k % RING)
            def both(t):
                return ps[:, 2 * t:2 * t + 2, :].rearrange("p b n -> p (b n)")

            act.wait_ge(mm_done, N_F + KC + RING)
            for t in range(TT):
                act.wait_ge(sqy_done, t)
                act.activation(scrap[:, :], both(t), ACT.Square, accum_out=st2[:, 0, t:t + 1]).then_inc(sqy_done, 1)
            act.wait_ge(stat, 1)
            act.activation(st2[:, 2, :], st2[:, 1, :], ACT.Sqrt).then_inc(sd_done, 1)
            for t in range(TT):
                act.wait_ge(x2_done, t + 1)
                act.wait_ge(sqx_done, t)
                act.activation(scrap[:, :], x2[:, t, :], ACT.Square, accum_out=st2[:, 3, t:t + 1]).then_inc(sqx_done, 1)
                if t == 1:
                    act.wait_ge(row_mm, 4)
                    act.activation(rows[:, 1, :], both(0), ACT.Copy).then_inc(b2_done, 1)
            act.wait_ge(stat, 3)
            act.activation(st2[:, 5, :], st2[:, 4, :], ACT.Sqrt).then_inc(sd_done, 1)
            for t in range(TT):
                act.wait_ge(h2_tr, t + 1)
                if t >= 2:
                    act.wait_ge(logit_mm, t - 1)
                b = (6, 0, 4, 6)[t]
                act.activation(h2T[:, t % 2, :, :].rearrange("p k n -> p (k n)"), ps[:, b:b + 2, :].rearrange("p b n -> p (b n)"),
                               ACT.Copy).then_inc(h2T_done, 1)
            act.wait_ge(negmax_done, 1)
            for t in range(TT):
                act.activation(ex[:, t, :], top[:, t, 0:TOP_K], ACT.Exp, bias=negmax[:, t:t + 1],
                               accum_out=exsum[:, t:t + 1]).then_inc(exp_done, 1)
            act.wait_ge(bst_full, 64)
            for r in range(3):
                act.activation(bias[:, r * D:(r + 1) * D], bst[:, r * D:(r + 1) * D], ACT.Copy).then_inc(bias_hi, 1)

            def c_hi_part(blk, q):
                c = SPLITS[q]
                act.wait_ge(craw_full[c // 2 % (RAW_RING // 2)], blk * 32 + (c // RAW_RING * 16 + 16))
                if q >= SPLIT_RING:
                    act.wait_ge(c_mm, blk * CH + (CH + SPLITS[q - SPLIT_RING] + 1))
                else:
                    act.wait_ge(c_mm, blk * CH + (SPLITS[q - SPLIT_RING + NS] + 1))
                act.activation(csplit[:, q % SPLIT_RING, 0, :], craw[c % RAW_RING], ACT.Copy).then_inc(c_hi, 1)

            def xe_high(blk, h):
                act.wait_ge(xe_tr, blk * 2 + (h + 1))
                act.activation(xe[:, 0, 4 * h:4 * h + 4, :].rearrange("p k n -> p (k n)"), ps[:, 4 + h, :], ACT.Copy).then_inc(xe_hi, 1)
                if h == 1:
                    act.activation(xe_w[:, :], ps[:, 5, 3 * P:4 * P], ACT.Copy).then_inc(xe_hi, 1)

            def sigmoid_gate(blk, h):
                act.wait_ge(gt_done, blk * 2 + (h + 1))
                act.wait_ge(act_done, blk * 2 + (h + 1))
                act.activation(sgm[:, :], gt[:, :], ACT.Sigmoid, scale=ALPHA).then_inc(sgm_done, 1)

            def ae_high(blk, h):
                act.wait_ge(ae_tr, blk * 2 + (h + 2))
                act.activation(ae[:, 0, 4 * h:4 * h + 4, :].rearrange("p k n -> p (k n)"), ps[:, 4 + h, :], ACT.Copy).then_inc(ae_hi, 1)
                act.activation(ae_w[:, h, :], ps[:, 4 + h, 3 * P:4 * P], ACT.Copy).then_inc(ae_hi, 1)

            def expert_begin(blk):
                for q in range(AHEAD):
                    c_hi_part(blk, q)
                for h in range(2):
                    xe_high(blk, h)

            def expert(blk, nxt):
                for q in range(AHEAD, NS):
                    c_hi_part(blk, q)
                    c = SPLITS[q]
                    if c == P_CHAIN0:
                        sigmoid_gate(blk, 0)
                    if c == P_AE0:
                        ae_high(blk, 0)
                    if c == P_CHAIN1:
                        sigmoid_gate(blk, 1)
                    if c == P_AE1:
                        ae_high(blk, 1)
                if nxt is not None:
                    xe_high(nxt, 0)
                    for q in range(AHEAD):
                        c_hi_part(nxt, q)
                    xe_high(nxt, 1)
                act.wait_ge(c_mm, blk * CH + 2 * CH)
                act.wait_ge(gate_ready, blk + 1)
                act.wait_ge(asg_ready, blk + 1)
                act.activation(yg[:, :], ps[:, 6:8, :].rearrange("p b n -> p (b n)"), ACT.Identity,
                               scale=gate_now[:, 0:1]).then_inc(yg_done, 1)

            expert_begin(0)
            with act.Fori(0, EXPERTS - 1) as j:
                expert(j, j + 1)
            expert(EXPERTS - 1, None)
            n_over = act.value_load(n_over_i[0:1, 0:1], min_val=0, max_val=MAX_OVER)
            with act.Fori(0, MAX_OVER) as j:
                with act.If(j < n_over):
                    expert_begin(j + EXPERTS)
                    expert(j + EXPERTS, None)
            for t in range(TT):
                act.wait_ge(sum_step, 3 * t + 3)
                act.wait_ge(sqz_done, t)
                act.activation(scrap2[:, :], yt[:, t, 0, :], ACT.Square, accum_out=st2[:, 0, t:t + 1]).then_inc(sqz_done, 1)
                act.wait_ge(stat3, 2 * t + 1)
                act.activation(st2[:, 2, t:t + 1], st2[:, 1, t:t + 1], ACT.Sqrt).then_inc(sd3_done, 1)


        @block.vector
        def _(dve):
            dve.memset(v[:, :, 0:CF_PAD], 0.0).then_inc(w_lo, RING)
            dve.memset(ones[:, :], 1.0).then_inc(bank_read, RING)
            dve.memset(mean_w[:, :], 1.0 / D).then_inc(ada_used, RING)
            dve.engine_nop().then_inc(c_lo, NS)
            dve.engine_nop().then_inc(clip_done, 2)
            dve.engine_nop().then_inc(act_done, 1)
            dve.wait_ge(ss_done, TT)
            dve.tensor_scalar(rs[:, :], ss[:, :], 1.0 / D, NORM_EPS, ALU.mult, ALU.add).then_inc(ms_done, 1)
            dve.wait_ge(sq_done, 1)
            dve.reciprocal(rs[:, :], rr[:, :]).then_inc(rs_done, 1)
            dve.wait_ge(rs_done, 1)
            for t in range(TT):
                dve.tensor_scalar(x_in[:, t, :], x_in[:, t, :], rs[:, t:t + 1], None, ALU.mult).then_inc(xn_done, 1)
            dve.wait_ge(sig_c, 1)
            dve.tensor_tensor(cact[:, :], pcol[:, :, R_C], csig[:, :], ALU.mult).then_inc(cact_done, 1)
            for g in range(POOLS):
                dve.memset(invw[:, 2 * g:2 * g + 2], 1.0 / (2 << g)).then_inc(pool_step, 1)
            dve.wait_ge(consts, 4)
            for k in range(KC):
                win = 2 << (k // 2)
                dve.tensor_scalar(corr[:, k, :], pos[:, :], float(win), 1.0 / win, ALU.min, ALU.mult).then_inc(pool_step, 1)
            dve.wait_ge(pool_step, POOLS + KC)
            dve.reciprocal(corr[:, :, :], corr[:, :, :]).then_inc(pool_step, 1)
            POOL0 = POOLS + KC + 1

            def lo(n, s, cols=D):
                dve.wait_ge(w_hi, n + 1)
                dve.tensor_tensor(split[:, s, 1, 0:cols], raw[:, s, 0:cols], split[:, s, 0, 0:cols].bitcast(F32),
                                  ALU.subtract).then_inc(w_lo, 1)

            dve.wait_ge(cact_done, 1)
            for k in range(KC):
                dve.wait_ge(ada1_full[k], 16)
                if k == 0:
                    dve.tensor_scalar(acc1[:, :], ada1[:, k, :], cact[:, k:k + 1], None, ALU.mult).then_inc(acc1_step, 1)
                else:
                    dve.wait_ge(acc1_step, k)
                    dve.scalar_tensor_tensor(acc1[:, :], ada1[:, k, :], cact[:, k:k + 1], acc1[:, :], ALU.mult, ALU.add).then_inc(acc1_step, 1)
            lo(0, 0)
            lo(1, 1)
            dve.wait_ge(mod_mm, 1)
            dve.tensor_tensor(mod1[:, :, :], ps[:, 7, 0:2 * KC].rearrange("p (a k) -> p a k", a=2),
                              pcol[:, :, R_SHIFT1:R_SHIFT1 + 2].rearrange("p k a -> p a k"), ALU.add).then_inc(mod_step, 1)
            dve.wait_ge(mod_step, 1)
            dve.scalar_tensor_tensor(mod1[:, 1, :], mod1[:, 1, :], 1.0, pcol[:, :, R_MIXG], ALU.add, ALU.mult).then_inc(mod_step, 1)
            dve.wait_ge(mod_step, 2)
            dve.wait_ge(xT_done, KC)
            for k in range(KC):
                dve.tensor_scalar(htmp[:, k, :], xT[:, k, :], mod1[:, 1, k:k + 1], mod1[:, 0, k:k + 1], ALU.mult, ALU.add).then_inc(h_f, 1)
                if k >= 1:
                    dve.wait_ge(h_hi, k)
                    dve.tensor_tensor(hT[:, 1, k - 1, :], htmp[:, k - 1, :], hT[:, 0, k - 1, :].bitcast(F32), ALU.subtract).then_inc(h_lo, 1)
            dve.wait_ge(h_hi, KC)
            dve.tensor_tensor(hT[:, 1, KC - 1, :], htmp[:, KC - 1, :], hT[:, 0, KC - 1, :].bitcast(F32), ALU.subtract).then_inc(h_lo, 1)
            dve.wait_ge(h_lo, KC)
            dve.memset(cxp[:, 0:SC_W - 1], 0.0).then_inc(pool_step, 1)
            dve.memset(csp[:, 0:SUM_PAD], 0.0).then_inc(pool_step, 1)
            POOL0 = POOL0 + 2

            conv_steps = [0]

            def taps(i, phase):
                for tap in range(*TAPS[phase]):
                    src = v[:, i, tap:tap + T]
                    wt = pcol[:, i, R_CF + tap:R_CF + tap + 1]
                    if tap == 0:
                        dve.tensor_scalar(cv[:, i, :], src, wt, pcol[:, i, R_CFB:R_CFB + 1], ALU.mult, ALU.add).then_inc(conv, 1)
                    else:
                        dve.wait_ge(conv, conv_steps[0])
                        dve.scalar_tensor_tensor(cv[:, i, :], src, wt, cv[:, i, :], ALU.mult, ALU.add).then_inc(conv, 1)
                    conv_steps[0] += 1

            for i in range(KC):
                n = N_A + 2 * i
                b = n % RING
                lo(n + 2, (n + 2) % RING)
                lo(n + 3, (n + 3) % RING)
                dve.wait_ge(sg_done, i + 1)
                dve.tensor_tensor(v[:, i, CF_PAD:CF_PAD + T], ps[:, b, :], sg[:, i % 2, :], ALU.mult).then_inc(bank_read, 2)
                dve.wait_ge(bank_read, n + 2 + RING)
                taps(i, "A")
            for i in range(KC):
                n = N_B + 4 * i
                lo(n + 2, 2)
                lo(n + 3, 3)
                dve.wait_ge(c_done, i + 1)
                dve.wait_ge(mm_done, n + 2 + RING)
                dve.tensor_tensor(cxp[:, SC_W - 1:SC_W - 1 + T], ps[:, 1, :], c_sb[:, :], ALU.mult).then_inc(bank_read, 2)
                dve.wait_ge(bank_read, n + 2 + RING)
                dve.wait_ge(s_hi, i)
                dve.tensor_scalar(t3[:, :], cxp[:, 0:T], pcol[:, i, R_SC:R_SC + 1], None, ALU.mult).then_inc(t3_step, 1)
                for a in range(1, SC_W):
                    dve.wait_ge(t3_step, i * SC_W + a)
                    dve.scalar_tensor_tensor(t3[:, :], cxp[:, a:a + T], pcol[:, i, R_SC + a:R_SC + a + 1], t3[:, :],
                                             ALU.mult, ALU.add).then_inc(t3_step, 1)
                lo(n + 4, 0)
                lo(n + 5, 1)
                dve.wait_ge(t3_step, i * SC_W + SC_W)
                dve.wait_ge(mm_done, n + 3 + RING)
                dve.tensor_tensor(t3[:, :], t3[:, :], ps[:, 2, :], ALU.mult).then_inc(s_f, 1)
                dve.wait_ge(mm_done, n + 4 + RING)
                dve.tensor_tensor_scan(csp[:, SUM_PAD:SUM_PAD + T], ps[:, 3, :], cxp[:, 0:T], 0.0, ALU.add, ALU.bypass).then_inc(pool_step, 1)
                dve.wait_ge(pool_step, i * 3 + (POOL0 + 1))
                win = 2 << (i // 2)
                dve.tensor_tensor(c_sb[:, :], csp[:, SUM_PAD:SUM_PAD + T], csp[:, SUM_PAD - win:SUM_PAD - win + T], ALU.subtract).then_inc(pool_step, 1)
                dve.wait_ge(pool_step, i * 3 + (POOL0 + 2))
                dve.tensor_tensor(c_sb[:, 0:MAX_WIN], c_sb[:, 0:MAX_WIN], corr[:, i, :], ALU.mult).then_inc(pool_step, 1)
                dve.wait_ge(pool_step, i * 3 + (POOL0 + 3))
                dve.scalar_tensor_tensor(pT[:, i, :], c_sb[:, :], invw[:, i:i + 1], ps[:, 3, :], ALU.mult, ALU.subtract).then_inc(bank_read, 2)
                dve.wait_ge(s_hi, i + 1)
                dve.tensor_tensor(sT[:, 1, i, :], t3[:, :], sT[:, 0, i, :].bitcast(F32), ALU.subtract).then_inc(s_lo, 1)
                taps(i, "B")
            for i in range(KC):
                n = N_C + 2 * i
                b = n % RING
                lo(n + 2, (n + 2) % RING)
                lo(n + 3, (n + 3) % RING)
                dve.wait_ge(sg_done, i + KC + 1)
                dve.wait_ge(mm_done, n + 2 + RING)
                dve.tensor_tensor(merged[:, i, :], ps[:, b + 1, :], sg[:, i % 2, :], ALU.mult).then_inc(bank_read, 2)
                taps(i, "C")
            for g in range(POOLS):
                n = N_D + 4 * g
                for h in range(2):
                    dve.wait_ge(p_hi, 2 * g + h + 1)
                    dve.tensor_tensor(pS[:, 1, h, :], pT[:, 2 * g + h, :], pS[:, 0, h, :].bitcast(F32), ALU.subtract).then_inc(p_lo, 1)
                lo(n + 2, 2)
                lo(n + 3, 3, 2 * P)
                for h in range(2):
                    m = 2 * g + h
                    dve.wait_ge(sg_done, 2 * KC + m + 1)
                    dve.wait_ge(mm_done, n + 2 * h + 2 + RING)
                    dve.wait_ge(mg_step, m)
                    dve.scalar_tensor_tensor(xtra[:, :], ps[:, 2 * h + 1, :], pcol[:, m, R_POOLS:R_POOLS + 1], sg[:, h, :],
                                             ALU.mult, ALU.mult).then_inc(bank_read, 2)
                    dve.wait_ge(bank_read, n + 2 * h + 2 + RING)
                    dve.tensor_tensor(merged[:, m, :], merged[:, m, :], xtra[:, :], ALU.add).then_inc(mg_step, 1)
                    if h == 0:
                        lo(n + 4, 0)
                        lo(n + 5, 1, 2 * P if g < POOLS - 1 else D)
                    taps(m, "D")

            def centre(k):
                dve.tensor_tensor(cv[:, k, :], cv[:, k, :], mu[:, :], ALU.subtract).then_inc(cen_done, 1)

            def silu(k):
                dve.wait_ge(z_done, 2 * k + 2)
                dve.tensor_tensor(cv[:, k, :], zl[:, k % 2, :], tmp[:, k % 2, :], ALU.mult).then_inc(vf_done, 1)

            def silu_lo(k):
                dve.wait_ge(v_hi, k + 1)
                dve.tensor_tensor(vT[:, 1, k, :], cv[:, k, :], vT[:, 0, k, :].bitcast(F32), ALU.subtract).then_inc(v_lo, 1)

            for i in range(KC):
                lo(N_E + i + 2, (i + 2) % RING)
                dve.wait_ge(g1_done, i + 1)
                dve.engine_nop().then_inc(bank_read, 1)
                if i == 1:
                    dve.wait_ge(mu_done, 1)
                    for k in range(4):
                        centre(k)
                if i == 2:
                    for k in range(4, KC):
                        centre(k)
                if i == 3:
                    dve.wait_ge(var_mm, KC)
                    dve.tensor_scalar(lrs[:, :], ps[:, 5, :], LN_EPS, None, ALU.add).then_inc(var_e, 1)
                    dve.wait_ge(lsd_done, 1)
                    dve.reciprocal(lrs[:, :], lrs[:, :]).then_inc(lrs_done, 1)
                    dve.wait_ge(lrs_done, 1)
                if i >= 4:
                    for k in range(2 * (i - 4), 2 * (i - 4) + 2):
                        dve.wait_ge(sq2_done, KC)
                        dve.tensor_tensor(cv[:, k, :], cv[:, k, :], lrs[:, :], ALU.mult).then_inc(xh_done, 1)
                        if k >= 1:
                            silu(k - 1)
                        if k >= 2:
                            silu_lo(k - 2)
            silu(KC - 1)
            silu_lo(KC - 2)
            silu_lo(KC - 1)

            def ada_sum(q):
                r, k = q // KC, q % KC
                dve.wait_ge(ada_full[q % RING], (q // RING + 1) * 16)
                if k == 0:
                    dve.tensor_scalar(rows[:, r, :], ada_ring[:, q % RING, :], cact[:, k:k + 1], None, ALU.mult).then_inc(ada_used, 1)
                else:
                    dve.wait_ge(ada_used, q + RING)
                    dve.scalar_tensor_tensor(rows[:, r, :], ada_ring[:, q % RING, :], cact[:, k:k + 1], rows[:, r, :],
                                             ALU.mult, ALU.add).then_inc(ada_used, 1)

            for i in range(KC):
                n = N_G + i
                lo(n + 2, (n + 2) % RING)
                dve.wait_ge(mm_done, n + 1 + RING)
                dve.wait_ge(mg_step, i + KC)
                gate = sgp[:, i, :] if i < KC - 1 else sg[:, 0, :]
                dve.scalar_tensor_tensor(xtra[:, :], ps[:, n % RING, :], pcol[:, i, R_CFOB:R_CFOB + 1], gate,
                                         ALU.add, ALU.mult).then_inc(bank_read, 1)
                dve.wait_ge(bank_read, n + 1 + RING)
                dve.tensor_tensor(merged[:, i, :], merged[:, i, :], xtra[:, :], ALU.add).then_inc(mg_step, 1)
                ada_sum(i)
                dve.wait_ge(m_hi, i + 1)
                dve.tensor_tensor(mT[:, 1, i, :], merged[:, i, :], mT[:, 0, i, :].bitcast(F32), ALU.subtract).then_inc(m_lo, 1)
            for k in range(KC):
                if k >= 2:
                    lo(N_F + k, k % RING)
                for q in range(3):
                    ada_sum(KC + 3 * k + q)
            dve.wait_ge(gbc_full, 48)
            dve.wait_ge(row_done, 2)
            dve.tensor_tensor(rows[:, 0, :], rows[:, 0, :], gbc[:, 0, :], ALU.mult).then_inc(g1_ready, 1)
            dve.wait_ge(sqy_done, TT)
            dve.tensor_scalar(st2[:, 1, :], st2[:, 0, :], 1.0 / D, NORM_EPS, ALU.mult, ALU.add).then_inc(stat, 1)
            dve.wait_ge(sd_done, 1)
            dve.reciprocal(st2[:, 0, :], st2[:, 2, :]).then_inc(stat, 1)
            dve.wait_ge(stat, 2)
            dve.wait_ge(x2_full, 16)
            dve.wait_ge(g1_ready, 1)
            for t in range(TT):
                y_t = ps[:, 2 * t:2 * t + 2, :].rearrange("p b n -> p (b n)")
                dve.scalar_tensor_tensor(ynorm[:, :], y_t, st2[:, 0, t:t + 1], rows[:, 0, :], ALU.mult, ALU.mult).then_inc(x2_step, 1)
                dve.wait_ge(x2_step, t + 1)
                dve.tensor_tensor(x2[:, t, :], x2[:, t, :], ynorm[:, :], ALU.add).then_inc(x2_done, 1)
                dve.wait_ge(x2_done, t + 1)
            dve.wait_ge(row_mm, 6)
            dve.scalar_tensor_tensor(rows[:, 2, :], ps[:, 2:4, :].rearrange("p b n -> p (b n)"), 1.0, gbc[:, 1, :],
                                     ALU.add, ALU.mult).then_inc(mod2_done, 1)
            dve.wait_ge(row_mm, 8)
            dve.tensor_tensor(rows[:, 3, :], ps[:, 4:6, :].rearrange("p b n -> p (b n)"), gbc[:, 2, :], ALU.mult).then_inc(mod2_done, 1)
            dve.wait_ge(sqx_done, TT)
            dve.tensor_scalar(st2[:, 4, :], st2[:, 3, :], 1.0 / D, NORM_EPS, ALU.mult, ALU.add).then_inc(stat, 1)
            dve.wait_ge(sd_done, 2)
            dve.reciprocal(st2[:, 3, :], st2[:, 5, :]).then_inc(stat, 1)
            dve.wait_ge(stat, 4)
            dve.wait_ge(mod2_done, 2)
            dve.wait_ge(b2_done, 1)
            for t in range(TT):
                dve.scalar_tensor_tensor(h2[:, t, :], x2[:, t, :], st2[:, 3, t:t + 1], rows[:, 2, :], ALU.mult, ALU.mult).then_inc(h2_step, 1)
                dve.wait_ge(h2_step, t + 1)
                dve.tensor_tensor(h2[:, t, :], h2[:, t, :], rows[:, 1, :], ALU.add).then_inc(h2_done, 1)

            n_r = [0]

            def step(ins):
                ins.then_inc(routed, 1)
                n_r[0] += 1
                dve.wait_ge(routed, n_r[0])

            dve.wait_ge(logit_mm, TT)
            dve.wait_ge(wr_full, 32)
            step(dve.tensor_tensor(logits[:, :, :], ps[:, 2, 0:TT * EXPERTS].rearrange("p (t e) -> p t e", t=TT),
                                   brt[:, :].unsqueeze(1).broadcast_to((P, TT, EXPERTS)), ALU.add))
            for t in range(TT):
                step(dve.max(top[:, t, :], logits[:, t, :]))
            dve.tensor_scalar(negmax[:, :], top[:, :, 0], -1.0, None, ALU.mult).then_inc(negmax_done, 1)
            for t in range(TT):
                step(dve.max_index(topi[:, t, :], top[:, t, :], logits[:, t, :]))
            step(dve.tensor_copy(idxf[:, :, :], topi[:, :, 0:TOP_K]))
            dve.wait_ge(consts2, 6)
            step(dve.tensor_tensor(onehots[:, :, :, :], iota_e[:, 0:EXPERTS].unsqueeze(1).unsqueeze(1).broadcast_to((P, TT, TOP_K, EXPERTS)),
                                   idxf[:, :, :].unsqueeze(3).broadcast_to((P, TT, TOP_K, EXPERTS)), ALU.is_equal))
            dve.tensor_reduce(mark[:, :, :], onehots[:, :, :, :].rearrange("p t k e -> p t e k"), AX.X, ALU.add).then_inc(mark_done, 1)
            dve.wait_ge(rank_mm, 2)
            step(dve.tensor_tensor(picked[:, :, :, :], onehots[:, :, :, :],
                                   ps[:, 3, 0:P].rearrange("p (t e) -> p t e", t=TT).unsqueeze(2).broadcast_to((P, TT, TOP_K, EXPERTS)), ALU.mult))
            step(dve.tensor_reduce(rank[:, :, :], picked[:, :, :, :], AX.X, ALU.add))
            step(dve.tensor_scalar(beyond[:, :, :], rank[:, :, :], float(P), None, ALU.is_ge))
            for b in range(2, TOP_K):
                step(dve.scalar_tensor_tensor(beyond[:, :, :], rank[:, :, :], float(b * P), beyond[:, :, :], ALU.is_ge, ALU.add))
            step(dve.tensor_scalar(place_f[:, :, :], rank[:, :, :], float(P), None, ALU.mult))
            step(dve.scalar_tensor_tensor(place_f[:, :, :], idxf[:, :, :], 4.0, place_f[:, :, :], ALU.mult, ALU.add))
            step(dve.scalar_tensor_tensor(place_f[:, :, :], beyond[:, :, :], float(1 - P * P), place_f[:, :, :], ALU.mult, ALU.add))
            dve.tensor_copy(place[:, :], place_f[:, :, :].rearrange("p t k -> p (t k)")).then_inc(place_ready, 1)
            dve.wait_ge(exp_done, TT)
            step(dve.reciprocal(exinv[:, :], exsum[:, :]))
            dve.tensor_tensor(pay[:, :, 1].rearrange("p (t k) -> p t k", t=TT).bitcast(F32), ex[:, :, :],
                              exinv[:, :].unsqueeze(2).broadcast_to((P, TT, TOP_K)), ALU.mult).then_inc(gates_ready, 1)
            step(dve.memset(flags[:, :, 0], 0.0))
            for b in range(1, 4):
                step(dve.tensor_scalar(flags[:, :, b], ps[:, 3, P:P + EXPERTS], float(b * P) + 0.5, None, ALU.is_ge))
            flat = flags[:, :, :].rearrange("p e b -> p (e b)")
            step(dve.tensor_tensor_scan(prefix[:, :], flat, flat, 0.0, ALU.add, ALU.bypass))
            step(dve.scalar_tensor_tensor(chosen[:, :], prefix[:, :], pidx[:, 0:1], flat, ALU.is_equal, ALU.mult))
            step(dve.tensor_tensor(chosen[:, :], chosen[:, :], iota_e[:, :], ALU.mult))
            dve.tensor_reduce(code[:, :], chosen[:, :], AX.X, ALU.add).then_inc(code_done, 1)
            dve.tensor_copy(n_over_i[0:1, 0:1], prefix[0:1, P - 1:P]).then_inc(codes_ready, 1)
            dve.wait_ge(code_mm, 1)
            dve.tensor_copy(code_row[0:1, :], ps[0:1, 3, 2 * P:2 * P + 16]).then_inc(codes_ready, 1)
            dve.wait_ge(bias_hi, 3)
            dve.tensor_tensor(bias[EXPERTS:2 * EXPERTS, :], bst[EXPERTS:2 * EXPERTS, :], bias[EXPERTS:2 * EXPERTS, :].bitcast(F32),
                              ALU.subtract).then_inc(bias_ready, 1)

            def c_lo_part(blk, q):
                c = SPLITS[q]
                dve.wait_ge(c_hi, blk * NS + (q + 1))
                dve.tensor_tensor(csplit[:, q % SPLIT_RING, 1, :], craw[c % RAW_RING],
                                  csplit[:, q % SPLIT_RING, 0, :].bitcast(F32), ALU.subtract).then_inc(c_lo, 1)

            def xe_low(blk, h):
                dve.wait_ge(xe_hi, blk * 3 + (2 * h + 1))
                dve.tensor_tensor(xe[:, 1, 4 * h:4 * h + 4, :].rearrange("p k n -> p (k n)"), ps[:, 4 + h, :],
                                  xe[:, 0, 4 * h:4 * h + 4, :].rearrange("p k n -> p (k n)").bitcast(F32), ALU.subtract).then_inc(xe_lo, 1)

            def ae_low(blk, h):
                dve.wait_ge(ae_hi, blk * 4 + (2 * h + 2))
                dve.tensor_tensor(ae[:, 1, 4 * h:4 * h + 4, :].rearrange("p k n -> p (k n)"), ps[:, 4 + h, :],
                                  ae[:, 0, 4 * h:4 * h + 4, :].rearrange("p k n -> p (k n)").bitcast(F32), ALU.subtract).then_inc(ae_lo, 1)

            def swiglu(blk, h):
                dve.wait_ge(c_mm, blk * CH + (CH + 8 * h + 8))
                dve.wait_ge(sgm_done, blk * 2 + (h + 1))
                dve.tensor_scalar(gt[:, :], ps[:, 2 * h, :], LIMIT, None, ALU.min).then_inc(gt_done, 1)
                dve.wait_ge(ae_tr, blk * 2 + (h + 1))
                dve.tensor_scalar(ua[:, :], ps[:, 2 * h + 1, :], -LIMIT, LIMIT, ALU.max, ALU.min).then_inc(clip_done, 1)
                dve.wait_ge(clip_done, blk * 2 + (h + 3))
                dve.scalar_tensor_tensor(ua[:, :], ua[:, :], 1.0, gt[:, :], ALU.add, ALU.mult).then_inc(up_done, 1)
                dve.wait_ge(up_done, blk * 2 + (h + 1))
                dve.wait_ge(sgm_done, blk * 2 + (h + 2))
                dve.tensor_tensor(ua[:, :], ua[:, :], sgm[:, :], ALU.mult).then_inc(act_done, 1)

            def expert_begin(blk):
                for q in range(AHEAD):
                    c_lo_part(blk, q)
                for h in range(2):
                    xe_low(blk, h)

            def expert(blk, nxt):
                for q in range(AHEAD, NS):
                    c_lo_part(blk, q)
                    c = SPLITS[q]
                    if c == P_CHAIN0:
                        swiglu(blk, 0)
                    if c == P_AE0:
                        ae_low(blk, 0)
                    if c == P_CHAIN1:
                        swiglu(blk, 1)
                    if c == P_AE1:
                        ae_low(blk, 1)
                if nxt is not None:
                    xe_low(nxt, 0)
                    for q in range(AHEAD):
                        c_lo_part(nxt, q)
                    xe_low(nxt, 1)

            for q in range(AHEAD):
                c_lo_part(0, q)
            dve.wait_ge(table_full, 16)
            dve.tensor_scalar(token_of[:, :], table[:, :, 0], 2, None, ALU.arith_shift_right).then_inc(tokens_ready, 1)
            for h in range(2):
                xe_low(0, h)
            with dve.Fori(0, EXPERTS - 1) as j:
                expert(j, j + 1)
            expert(EXPERTS - 1, None)
            n_over = dve.value_load(n_over_i[0:1, 0:1], min_val=0, max_val=MAX_OVER)
            with dve.Fori(0, MAX_OVER) as j:
                with dve.If(j < n_over):
                    expert_begin(j + EXPERTS)
                    expert(j + EXPERTS, None)
            def last_norm(t):
                dve.wait_ge(sqz_done, t + 1)
                dve.tensor_scalar(st2[:, 1, t:t + 1], st2[:, 0, t:t + 1], 1.0 / D, NORM_EPS, ALU.mult, ALU.add).then_inc(stat3, 1)
                dve.wait_ge(sd3_done, t + 1)
                dve.reciprocal(st2[:, 3, t:t + 1], st2[:, 2, t:t + 1]).then_inc(stat3, 1)
                dve.wait_ge(stat3, 2 * t + 2)
                dve.scalar_tensor_tensor(yt[:, t, 1, :], yt[:, t, 0, :], st2[:, 3, t:t + 1], rows[:, 3, :], ALU.mult, ALU.mult).then_inc(out_step, 1)
                dve.wait_ge(out_step, t + 1)
                dve.tensor_tensor(x2[:, t, :], x2[:, t, :], yt[:, t, 1, :], ALU.add).then_inc(out_ready, 1)

            for t in range(TT):
                dve.wait_ge(yt_full[t], 16)
                for k in range(1, TOP_K):
                    dve.wait_ge(sum_step, 3 * t + k - 1)
                    dve.tensor_tensor(yt[:, t, 0, :], yt[:, t, 0, :], yt[:, t, k, :], ALU.add).then_inc(sum_step, 1)
                if t >= 1:
                    last_norm(t - 1)
            last_norm(TT - 1)


        @block.gpsimd
        def _(pool):
            pool.engine_nop().then_inc(sgm_done, 1)
            pool.engine_nop().then_inc(yg_done, 1)
            pool.iota(table[:, :, 0], pattern=[[0, P]], base=NO_ROW, channel_multiplier=0).then_inc(table_set, 1)
            pool.iota(table[:, :, 1], pattern=[[0, P]], base=0, channel_multiplier=0).then_inc(table_set, 1)
            pool.wait_ge(table_set, 2)
            pool.dma_start(table_d.rearrange("(p e) w -> p e w", p=P), table[:, :, :]).then_inc(table_cleared, 16)
            pool.memset(ident[:, :], 0.0).then_inc(consts, 1)
            pool.wait_ge(consts, 1)
            pool.affine_select(out=ident[:, :], in_=ident[:, :], compare_op=ALU.not_equal, fill=1.0, base=0,
                               pattern=[[-1, P]], channel_multiplier=1).then_inc(consts, 1)
            pool.iota(pos_i[:, :], pattern=[[1, MAX_WIN]], base=1, channel_multiplier=0).then_inc(consts, 1)
            pool.wait_ge(consts, 3)
            pool.tensor_copy(pos[:, :], pos_i[:, :]).then_inc(consts, 1)
            pool.wait_ge(v_lo, KC)
            with pool.Fori(0, 4) as j:
                for k in range(KC):
                    pool.wait_ge(ada_used, j * 8 + (k + 1))
                    pool.dma_start(ada_ring[:, k % RING, :], ada_w[0, k * P:(k + 1) * P, ds(j * D + 2 * D, D)]).then_inc(ada_full[k % RING], 16)
            pool.wait_ge(m_lo, KC)
            pool.iota(iota_i[:, :], pattern=[[1, P]], base=0, channel_multiplier=0).then_inc(consts2, 1)
            pool.iota(pidx_i[:, :], pattern=[[0, 1]], base=1, channel_multiplier=1).then_inc(consts2, 1)
            pool.wait_ge(consts2, 2)
            pool.tensor_copy(iota_e[:, :], iota_i[:, :]).then_inc(consts2, 1)
            pool.tensor_copy(pidx[:, :], pidx_i[:, :]).then_inc(consts2, 1)
            pool.affine_select(out=tri[:, :], in_=ones[:, :], compare_op=ALU.is_gt, fill=0.0, base=0,
                               pattern=[[1, P]], channel_multiplier=-1).then_inc(consts2, 1)
            pool.iota(pay[:, :, 0], pattern=[[P * TOP_K, TT], [1, TOP_K]], base=0, channel_multiplier=TOP_K).then_inc(consts2, 1)
            pool.wait_ge(consts2, 6)
            pool.tensor_copy(eye2[0:EXPERTS, :], ident[0:EXPERTS, 0:EXPERTS]).then_inc(consts2, 1)
            pool.wait_ge(consts2, 7)
            pool.tensor_copy(eye2[EXPERTS:2 * EXPERTS, :], ident[EXPERTS:2 * EXPERTS, EXPERTS:2 * EXPERTS]).then_inc(consts2, 1)
            pool.wait_ge(h2_stored, TT * 16)
            pool.wait_ge(h2_tr, TT)
            pool.wait_ge(consts2, 8)
            pool.memset(fence[:, :], 0.0).then_inc(consts2, 1)
            pool.wait_ge(consts2, 9)
            pool.memset(xg[:, :], 0.0).then_inc(consts2, 1)
            pool.wait_ge(place_ready, 1)
            pool.wait_ge(gates_ready, 1)
            pool.wait_ge(table_cleared, 16)
            pool.wait_ge(consts2, 10)
            for a in range(TT * TOP_K):
                pool.indirect_dma_start(out=table_d, out_offset=bass.IndirectOffsetOnAxis(ap=place[:, a:a + 1], axis=0),
                                        in_=pay[:, a, :], in_offset=None).then_inc(table_put, 16)
            pool.wait_ge(table_put, TT * TOP_K * 16)
            pool.dma_start(table[:, :, :], table_d.rearrange("(p e) w -> p e w", p=P)).then_inc(table_full, 16)
            pool.wait_ge(tokens_ready, 1)

            last_token, last_row = pool.to_reg(T - 1), pool.to_reg(T * TOP_K - 1)

            def gather(blk, col):
                pool.wait_ge(xg_full, blk * 16)
                pool.tensor_copy(tok_now[:, :], token_of[:, ds(col, 1)]).then_inc(tok_ready, 1)
                pool.wait_ge(tok_ready, blk + 1)
                pool.wait_ge(xe_tr, blk * 2)
                pool.tensor_tensor(fence[:, 0:1], fence[:, 1:2], fence[:, 1:2], ALU.add)
                pool.indirect_dma_start(out=xg[:, :], out_offset=None, in_=h2_rows,
                                        in_offset=bass.IndirectOffsetOnAxis(ap=tok_now[:, 0:1], axis=0),
                                        bounds_check=last_token, oob_is_err=False).then_inc(xg_full, 16)

            def choose(blk, e):
                pool.wait_ge(hot_used, blk)
                pool.tensor_copy(hot[:, :], eye2[:, ds(e, 1)].broadcast_to((2 * EXPERTS, P))).then_inc(hot_ready, 1)

            def labels(blk, col):
                pool.wait_ge(yg_done, blk + 1)
                pool.tensor_copy(gate_now[:, :], table[:, ds(col, 1), 1].bitcast(F32)).then_inc(gate_ready, 1)
                pool.wait_ge(y_put, blk * 16)
                pool.tensor_copy(asg_now[:, :], table[:, ds(col, 1), 0]).then_inc(asg_ready, 1)

            def scatter(blk):
                pool.wait_ge(yg_done, blk + 2)
                pool.wait_ge(asg_ready, blk + 1)
                pool.tensor_tensor(fence[:, 2:3], fence[:, 1:2], fence[:, 1:2], ALU.add)
                pool.indirect_dma_start(out=y_rows, out_offset=bass.IndirectOffsetOnAxis(ap=asg_now[:, 0:1], axis=0),
                                        in_=yg[:, :], in_offset=None,
                                        bounds_check=last_row, oob_is_err=False).then_inc(y_put, 16)

            gather(0, 0)
            choose(0, 0)
            labels(0, 0)
            with pool.Fori(0, EXPERTS - 1) as j:
                gather(j + 1, j * 4 + 4)
                choose(j + 1, j + 1)
                scatter(j)
                labels(j + 1, j * 4 + 4)
            scatter(EXPERTS - 1)
            pool.wait_ge(codes_ready, 2)
            n_over = pool.value_load(n_over_i[0:1, 0:1], min_val=0, max_val=MAX_OVER)
            with pool.Fori(0, MAX_OVER) as j:
                with pool.If(j < n_over):
                    code_j = pool.value_load(code_row[0:1, ds(j, 1)], min_val=0, max_val=P - 1)
                    gather(j + EXPERTS, code_j)
                    choose(j + EXPERTS, code_j // 4)
                    labels(j + EXPERTS, code_j)
                    scatter(j + EXPERTS)
                    pool.wait_ge(y_put, j * 16 + (EXPERTS + 1) * 16)
            pool.wait_ge(y_put, EXPERTS * 16)
            pool.engine_nop().then_inc(moe_done, 1)


        @block.tensor
        def _(pe):
            pe.wait_ge(consts, 2)
            pe.matmul(ps[:, 6, 0:1], ident[:, :], ident[:, 0:1], start=True, stop=True).then_inc(mm_done, RING)
            pe.matmul(ps[:, 6, 1:2], ident[:, :], ident[:, 0:1], start=True, stop=True).then_inc(c_mm, CH)
            pe.matmul(ps[:, 6, 2:3], ident[:, :], ident[:, 0:1], start=True, stop=True).then_inc(ae_tr, 1)
            pe.wait_ge(prow_full, 160)
            for k in range(KC):
                last = pe.transpose(ps[:, 0, k * N_ROWS:(k + 1) * N_ROWS], prow[0:N_ROWS, k * P:(k + 1) * P], ident[0:N_ROWS, 0:N_ROWS])
            last.then_inc(pcol_mm, 1)
            pe.wait_ge(xn_done, TT)
            for k in range(KC):
                if k >= 4:
                    pe.wait_ge(xT_done, k - 3)
                for t in range(TT):
                    last = pe.transpose(ps[:, 1 + k % 4, t * P:(t + 1) * P], x_in[:, t, k * P:(k + 1) * P], ident[:, :])
                last.then_inc(xT_mm, 1)
            pe.wait_ge(acc1_step, KC)
            for m in range(2 * KC):
                last = pe.matmul(ps[:, 7, m:m + 1], acc1[:, m * P:(m + 1) * P], ones[:, 0:1], start=True, stop=True)
            last.then_inc(mod_mm, 1)

            def block(n, s, moving, ks=range(KC)):
                pe.wait_ge(w_lo, n + (1 + RING))
                pe.wait_ge(bank_read, n + 1)
                for kk, k in enumerate(ks):
                    w_hi_k = split[:, s, 0, kk * P:(kk + 1) * P]
                    w_lo_k = split[:, s, 1, kk * P:(kk + 1) * P]
                    pe.matmul(ps[:, s, :], w_hi_k, moving[:, 0, k, :], start=(kk == 0), stop=False)
                    pe.matmul(ps[:, s, :], w_hi_k, moving[:, 1, k, :], start=False, stop=False)
                    last = pe.matmul(ps[:, s, :], w_lo_k, moving[:, 0, k, :], start=False, stop=(kk == len(ks) - 1))
                last.then_inc(mm_done, 1)

            pe.wait_ge(h_lo, KC)
            with pe.Fori(0, 4) as j:
                for s in range(RING):
                    block(j * 4 + (N_A + s), s, hT)
            with pe.Fori(0, 8) as i:
                for s in range(RING):
                    block(i * 4 + (N_B + s), s, hT)
            pe.wait_ge(s_lo, KC)
            with pe.Fori(0, 4) as j:
                for s in range(RING):
                    block(j * 4 + (N_C + s), s, hT if s % 2 == 0 else sT)
            for g in range(POOLS):
                for s in range(RING):
                    if s == 1:
                        pe.wait_ge(p_lo, 2 * g + 2)
                    if s % 2 == 0:
                        block(N_D + 4 * g + s, s, hT)
                    else:
                        block(N_D + 4 * g + s, s, pS, range(2))
            def gate_block(i):
                block(N_E + i, i % RING, hT)

            gate_block(0)
            pe.wait_ge(conv, KC * CF_W)
            for k in range(KC):
                last = pe.matmul(ps[:, 4, :], mean_w[:, :], cv[:, k, :], start=(k == 0), stop=(k == KC - 1))
            last.then_inc(mean_mm, 1)
            gate_block(1)
            gate_block(2)
            for k in range(KC):
                pe.wait_ge(sq2_done, k + 1)
                pe.matmul(ps[:, 5, :], mean_w[:, :], sq[:, k % 2, :], start=(k == 0), stop=(k == KC - 1)).then_inc(var_mm, 1)
            for i in range(3, KC):
                gate_block(i)
            pe.wait_ge(v_lo, KC)
            with pe.Fori(0, 2) as j:
                for s in range(RING):
                    block(j * 4 + (N_G + s), s, vT)

            def row_sum(r, b):
                bias_row = brow0[0:1, :] if r == 0 else brow[0:1, r - 1, :]
                for h in range(2):
                    pe.matmul(ps[:, b + h, :], ones[:, :], rows[:, r, h * HALF:(h + 1) * HALF], start=True, stop=False)
                    pe.matmul(ps[:, b + h, :], ones[0:1, :], bias_row[:, h * HALF:(h + 1) * HALF], start=False, stop=True).then_inc(row_mm, 1)

            pe.wait_ge(ada_used, KC + RING)
            pe.wait_ge(brow0_full, 16)
            row_sum(0, 4)
            pe.wait_ge(bank_read, N_F + RING)
            for k in range(KC):
                s = k % RING
                pe.wait_ge(w_lo, N_F + k + 1 + RING)
                pe.wait_ge(m_lo, k + 1)
                for t in range(TT):
                    if k == 0 and t == 2:
                        pe.wait_ge(row_done, 2)
                    for h in range(2):
                        o_ = ps[:, 2 * t + h, :]
                        w_h, w_l = (split[:, s, a, h * HALF:(h + 1) * HALF] for a in range(2))
                        m_h, m_l = (mT[:, a, k, t * P:(t + 1) * P] for a in range(2))
                        pe.matmul(o_, m_h, w_h, start=(k == 0), stop=False)
                        pe.matmul(o_, m_h, w_l, start=False, stop=False)
                        last = pe.matmul(o_, m_l, w_h, start=False, stop=(k == KC - 1))
                last.then_inc(mm_done, 1)
            def router(t):
                pe.wait_ge(h2T_done, t + 1)
                if t == 0:
                    pe.wait_ge(mod2_done, 1)
                for k in range(KC):
                    last = pe.matmul(ps[:, 2, t * EXPERTS:(t + 1) * EXPERTS], h2T[:, t % 2, k, :], wr[:, k, :], start=(k == 0), stop=(k == KC - 1))
                last.then_inc(logit_mm, 1)

            pe.wait_ge(brow_full, 16)
            pe.wait_ge(ada_used, 4 * KC + RING)
            for r in range(1, 4):
                pe.wait_ge(x2_done, r)
                row_sum(r, 2 * r - 2)
            pe.wait_ge(wr_full, 32)
            for t in range(TT):
                b = (6, 0, 4, 6)[t]
                pe.wait_ge(h2_done, t + 1)
                if t == 3:
                    pe.wait_ge(h2T_done, 1)
                for k in range(KC):
                    last = pe.transpose(ps[:, b + k // 4, k % 4 * P:(k % 4 + 1) * P], h2[:, t, k * P:(k + 1) * P], ident[:, :])
                last.then_inc(h2_tr, 1)
                if t >= 1:
                    router(t - 1)
            router(TT - 1)
            pe.wait_ge(mark_done, 1)
            for t in range(TT):
                o_ = ps[:, 3, t * EXPERTS:(t + 1) * EXPERTS]
                for u in range(t):
                    pe.matmul(o_, ones[:, :], mark[:, u, :], start=(u == 0), stop=False)
                last = pe.matmul(o_, tri[:, :], mark[:, t, :], start=(t == 0), stop=True)
            last.then_inc(rank_mm, 1)
            for t in range(TT):
                last = pe.matmul(ps[:, 3, P:P + EXPERTS], ones[:, :], mark[:, t, :], start=(t == 0), stop=(t == TT - 1))
            last.then_inc(rank_mm, 1)
            pe.wait_ge(code_done, 1)
            pe.matmul(ps[0:1, 3, 2 * P:3 * P], code[:, 0:1], ident[:, :], start=True, stop=True).then_inc(code_mm, 1)

            def rows_of(k):
                first = k // 2 * 2 * P + k % 2
                return slice(first, first + 2 * P - 1, 2)

            def chunk(blk, c):
                if c < 16:
                    stand, stand_w, k, b = xe, xe_w[:, :], c % 8, c // 8 * 2
                else:
                    stand, stand_w, k, b = ae, ae_w[:, (c - 16) // 4, :], c - 16, 6
                end = k == 7
                if c in WHOLE:
                    pe.wait_ge(craw_full[c // 2 % (RAW_RING // 2)], blk * 32 + (c // RAW_RING * 16 + 16))
                    for u in range(2):
                        last = pe.matmul(ps[:, b + u, :], stand_w, craw[c % RAW_RING][:, u * HALF:(u + 1) * HALF], start=False, stop=end)
                else:
                    q = SPLITS.index(c)
                    s = q % SPLIT_RING
                    pe.wait_ge(c_lo, blk * NS + (NS + q + 1))
                    for a, parts in ((0, (0, 1)), (1, (0,))):
                        for u in range(2):
                            for w in parts:
                                last = pe.matmul(ps[:, b + u, :], stand[:, a, k, :], csplit[:, s, w, u * HALF:(u + 1) * HALF],
                                                 start=False, stop=(end and a == 1))
                last.then_inc(c_mm, 1)

            def biases(banks, cols):
                for b, col in zip(banks, cols):
                    last = pe.matmul(ps[:, b, :], hot[:, :], bias[:, col:col + HALF], start=True, stop=False)
                return last

            def turn_tokens(blk, h):
                if h == 0:
                    pe.wait_ge(xg_full, blk * 16 + 16)
                for i in range(4):
                    k = 4 * h + i
                    last = pe.transpose(ps[:, 4 + h, i * P:(i + 1) * P], xg[:, rows_of(k)], ident[:, :])
                last.then_inc(xe_tr, 1)

            def turn_acts(blk, h):
                pe.wait_ge(act_done, blk * 2 + (h + 2))
                for i in range(4):
                    last = pe.transpose(ps[:, 4 + h, i * P:(i + 1) * P], ua[:, rows_of(i)], ident[:, :])
                last.then_inc(ae_tr, 1)

            def expert(blk, nxt):
                pe.wait_ge(hot_ready, blk + 1)
                pe.wait_ge(clip_done, blk * 2 + 1)
                biases((0, 1), (0, D))
                pe.wait_ge(xe_lo, blk * 2 + 1)
                for c in range(4):
                    chunk(blk, c)
                pe.wait_ge(xe_lo, blk * 2 + 2)
                pe.wait_ge(xe_hi, blk * 3 + 3)
                for c in range(4, 8):
                    chunk(blk, c)
                pe.wait_ge(clip_done, blk * 2 + 2)
                biases((2, 3), (HALF, D + HALF))
                for c in range(8, 12):
                    chunk(blk, c)
                turn_acts(blk, 0)
                for c in range(12, 16):
                    chunk(blk, c)
                pe.wait_ge(yg_done, blk + 1)
                biases((6, 7), (2 * D, 2 * D + HALF)).then_inc(hot_used, 1)
                pe.wait_ge(ae_lo, blk * 2 + 1)
                pe.wait_ge(ae_hi, blk * 4 + 2)
                for c in range(16, 20):
                    chunk(blk, c)
                turn_acts(blk, 1)
                if nxt is not None:
                    turn_tokens(nxt, 0)
                pe.wait_ge(ae_lo, blk * 2 + 2)
                pe.wait_ge(ae_hi, blk * 4 + 4)
                for c in range(20, 24):
                    chunk(blk, c)
                if nxt is not None:
                    turn_tokens(nxt, 1)

            pe.wait_ge(bias_ready, 1)
            for h in range(2):
                turn_tokens(0, h)
            with pe.Fori(0, EXPERTS - 1) as j:
                expert(j, j + 1)
            expert(EXPERTS - 1, None)
            n_over = pe.value_load(n_over_i[0:1, 0:1], min_val=0, max_val=MAX_OVER)
            with pe.Fori(0, MAX_OVER) as j:
                with pe.If(j < n_over):
                    for h in range(2):
                        turn_tokens(j + EXPERTS, h)
                    expert(j + EXPERTS, None)


_INS = ["x", "c", "ada_w", "ada_b", "mix_pre_g", "mix_post_g", "w_in", "sc_conv", "sc_out", "cf_conv", "cf_conv_b",
        "cf_ln_g", "cf_ln_b", "cf_out", "cf_out_b", "pool_w", "pool_scale", "w_o", "moe_pre_g", "moe_post_g",
        "w_router", "b_router", "w_gu", "b_gu", "w_down", "b_down"]
_OUTS = [((1, 512, 1024), "float32")]


def kernel(**inputs):
    import numpy as _np
    import concourse.bacc as _bacc
    from concourse import mybir as _mybir
    from concourse.bass_utils import run_bass_kernel_spmd as _run

    nc = _bacc.Bacc("TRN2", target_bir_lowering=False, num_devices=1)
    arrays, args = {}, []
    for name in _INS:
        a = _np.ascontiguousarray(inputs[name])
        arrays[f"in_{name}_dram"] = a
        args.append(nc.dram_tensor(f"in_{name}_dram", a.shape, _mybir.dt.from_np(a.dtype), kind="ExternalInput").ap())
    for i, (shape, dtype) in enumerate(_OUTS):
        dt = _mybir.dt.from_np(_np.dtype(dtype))
        args.append(nc.dram_tensor(f"out_{i}_dram", shape, dt, kind="ExternalOutput").ap())
    build(nc, *args)
    r = _run(nc, [arrays], core_ids=[0])
    got = tuple(r.results[0][f"out_{i}_dram"] for i in range(len(_OUTS)))
    return got[0]
```

```python
from contextlib import ExitStack

import concourse.bass as bass
from concourse import mybir

ALU = mybir.AluOpType
ACT = mybir.ActivationFunctionType
AX = mybir.AxisListType
F32 = mybir.dt.float32
F32R = mybir.dt.float32r
I32 = mybir.dt.int32
U32 = mybir.dt.uint32
ds = bass.ds

P = 128
D = 1024
T = 512
KC = D // P
TT = T // P
HALF = 512
EXPERTS = 32
TOP_K = 4
NORM_EPS = 1e-6
LN_EPS = 1e-5
LIMIT = 7.0
ALPHA = 1.702
SC_W = 3
CF_W = 31
CF_PAD = CF_W - 1
POOLS = 4
MAX_WIN = 16
SUM_PAD = 32

R_C, R_MIXG, R_SHIFT1, R_SCALE1, R_CFB, R_LNG, R_LNB, R_CFOB, R_POOLS, R_SC = 0, 1, 2, 3, 4, 5, 6, 7, 8, 9
R_CF = R_SC + SC_W
N_ROWS = R_CF + CF_W

RING = 4
N_A, N_B, N_C, N_D, N_E, N_G, N_F = 0, 16, 48, 64, 80, 88, 96
TAPS = {"A": (0, 9), "B1": (9, 15), "B2": (15, 19), "C1": (19, 23), "C2": (23, 28), "D": (28, CF_W)}

CH = 24
RAW_RING = 12
SPLIT_RING = 10
WHOLE = (14, 15, 19, 23)
SPLITS = [c for c in range(CH) if c not in WHOLE]
NS = len(SPLITS)
POOL_LO = range(3, 6)
AHEAD = 4
P_CHAIN0, P_AE0, P_CHAIN1, P_AE1 = 12, 13, 18, 20


def splits_before(c):
    return sum(s < c for s in SPLITS)


MAX_OVER = T * TOP_K // P - 1
NO_ROW = 4 * T * TOP_K


def build(nc, x, cond, ada_w, ada_b, mix_pre_g, mix_post_g, w_in, sc_conv, sc_out, cf_conv, cf_conv_b,
          cf_ln_g, cf_ln_b, cf_out, cf_out_b, pool_w, pool_scale, w_o, moe_pre_g, moe_post_g,
          w_router, b_router, w_gu, b_gu, w_down, b_down, out):
    with ExitStack() as ctx:
        KB = 1024
        base = (nc.sbuf_base + 63) // 64 * 64

        def at(name, off, shape, dt=F32):
            return nc.alloc_sbuf_tensor_at(name, shape, dt, offset=base + off)

        def sem(name):
            return ctx.enter_context(nc.semaphore(name))

        o_merged, o_rows, o_v, o_p, o_cv, o_ht, o_s, o_raw, o_split, o_misc = (
            0, 16 * KB, 32 * KB, 49 * KB, 65 * KB, 81 * KB, 113 * KB, 145 * KB, 161 * KB, 193 * KB)
        x_in = at("x_in", o_rows, [P, TT, D])
        prow = at("prow", o_merged, [P, D])
        xT = at("xT", o_p, [P, KC, T])
        ada1 = at("ada1", o_ht, [P, KC, 2 * D])
        hT = at("hT", o_ht, [P, 2, KC, T], F32R)
        htmp = at("htmp", o_merged, [P, KC, T])
        v = at("v", o_v, [P, KC, CF_PAD + T])
        cv = at("cv", o_cv, [P, KC, T])
        sT = at("sT", o_s, [P, 2, KC, T], F32R)
        pT = at("pT", o_p, [P, KC, T])
        c_sb = at("c_sb", o_merged + 4 * KB, [P, T])
        cxp = at("cxp", o_merged + 6 * KB, [P, SC_W - 1 + T])
        t3 = at("t3", o_merged + 9 * KB, [P, T])
        csp = at("csp", o_merged + 11 * KB + 256, [P, SUM_PAD + T])
        merged = at("merged", o_merged, [P, KC, T])
        pS = at("pS", o_s, [P, 2, 2, T], F32R)
        acc1 = at("acc1", o_cv, [P, 2 * D])
        sgp = at("sgp", o_p + KB, [P, KC - 1, T])
        mu = at("mu", o_v, [P, T])
        lrs = at("lrs", o_v + 2 * KB, [P, T])
        sq = at("sq", o_v + 4 * KB, [P, 2, T])
        zl = at("zl", o_v + 8 * KB, [P, 2, T])
        vT = at("vT", o_s, [P, 2, KC, T], F32R)
        mT = at("mT", o_v, [P, 2, KC, T], F32R)
        ada_ring = at("ada_ring", o_cv, [P, RING, D])
        rows = at("rows", o_rows, [P, 4, D])
        raw = at("raw", o_raw, [P, RING, D])
        split = at("split", o_split, [P, RING, 2, D], F32R)
        pcol = at("pcol", o_misc, [P, KC, N_ROWS])
        o = o_misc + 1408
        ident = at("ident", o, [P, P]); o += 512
        mean_w = at("mean_w", o, [P, P]); o += 512
        ones = at("ones", o, [P, P]); o += 512
        sg = at("sg", o, [P, 2, T]); o += 4 * KB
        tmp = at("tmp", o, [P, 2, T]); o += 4 * KB
        corr = at("corr", o, [P, KC, MAX_WIN]); o += 512
        invw = at("invw", o, [P, KC]); o += 32
        pos = at("pos", o, [P, MAX_WIN]); o += 64
        pos_i = at("pos_i", o, [P, MAX_WIN], I32); o += 64
        xtra = at("xtra", o, [P, T]); o += 2 * KB
        cact = at("cact", o, [P, KC]); o += 32
        csig = at("csig", o, [P, KC]); o += 32
        mod1 = at("mod1", o, [P, 2, KC]); o += 64
        ss = at("ss", o, [P, TT]); o += 32
        rs = at("rs", o, [P, TT]); o += 32
        rr = at("rr", o, [P, TT]); o += 32

        ps = ctx.enter_context(nc.psum_tensor("ps", [P, 8, HALF], F32))

        o_2 = o_v
        x2 = at("x2", o_merged, [P, TT, D])
        bias = at("bias", o_rows, [2 * EXPERTS, 3 * D], F32R)
        h2 = at("h2", o_2, [P, TT, D])
        scrap = at("scrap", o_2 + 16 * KB, [P, D])
        ynorm = at("ynorm", o_2 + 20 * KB, [P, D])
        h2T = at("h2T", o_2 + 24 * KB, [P, 2, KC, P])
        brow0 = rows[0:1, 1, :]
        ada_ring0 = at("ada_ring0", o_s + 8 * KB, [P, RING, D])
        brow = at("brow", o_s, [1, 3, D])
        gbc = at("gbc", o_s + 12 * KB, [P, 3, D])
        bst = at("bst", o_s + 64 * KB, [2 * EXPERTS, 3 * D])
        xg = at("xg", o_2, [P, D])
        yg = at("yg", o_2 + 4 * KB, [P, D])
        xe = at("xe", o_2 + 8 * KB, [P, 2, KC, P], F32R)
        ae = at("ae", o_2 + 16 * KB, [P, 2, KC, P], F32R)
        craw2 = [at(f"craw2_{p}", (o_ht + p * 8 * KB) if p < 4 else o_cv + (p - 4) * 8 * KB, [P, 2, D]) for p in range(RAW_RING // 2)]
        craw = [craw2[s // 2][:, s % 2, :] for s in range(RAW_RING)]
        csplit = at("csplit", o_s, [P, SPLIT_RING, 2, D], F32R)
        scrap2 = at("scrap2", o_2, [P, D])
        yt = at("yt", o_ht, [P, TT, TOP_K, D])
        o = o_2 + 24 * KB
        gt = at("gt", o, [P, HALF]); o += 2 * KB
        sgm = at("sgm", o, [P, HALF]); o += 2 * KB
        ua = at("ua", o, [P, HALF]); o += 2 * KB
        xe_w = at("xe_w", o, [P, 2, P]); o += 1024
        ae_w = at("ae_w", o, [P, 2, P]); o += 1024
        o = o_misc + 1408 + 1536
        wr = at("wr", o, [P, KC, EXPERTS]); o += KB
        brt = at("brt", o, [P, EXPERTS]); o += 128
        iota_e = at("iota_e", o, [P, P]); o += 512
        tri = at("tri", o, [P, P]); o += 512
        eye2 = at("eye2", o, [2 * EXPERTS, EXPERTS]); o += 128
        pidx_i = at("pidx_i", o, [P, 1], I32); o += 32
        pidx = at("pidx", o, [P, 1]); o += 32
        logits = at("logits", o, [P, TT, EXPERTS]); o += 512
        assert o <= o_misc + 1408 + 1536 + 4 * KB
        o = o_misc + 1408 + 1536 + 4 * KB
        top = at("top", o, [P, TT, 8]); o += 128
        topi = at("topi", o, [P, TT, 8], U32); o += 128
        negmax = at("negmax", o, [P, TT]); o += 32
        ex = at("ex", o, [P, TT, TOP_K]); o += 64
        exsum = at("exsum", o, [P, TT]); o += 32
        exinv = at("exinv", o, [P, TT]); o += 32
        idxf = at("idxf", o, [P, TT, TOP_K]); o += 64
        rank = at("rank", o, [P, TT, TOP_K]); o += 64
        beyond = at("beyond", o, [P, TT, TOP_K]); o += 64
        column = at("column", o, [P, TT, TOP_K]); o += 64
        gates = at("gates", o, [P, TT, TOP_K]); o += 64
        number_i = at("number_i", o, [P, TT, TOP_K], I32); o += 64
        number = at("number", o, [P, TT * TOP_K]); o += 64
        before = at("before", o_2 + 20 * KB + 1024, [P, TT + 1, EXPERTS])
        lT = at("lT", o_2 + 20 * KB, [EXPERTS, 2, P])
        mark = at("mark", o, [P, TT, EXPERTS]); o += 512
        flags = at("flags", o, [P, EXPERTS, 4]); o += 512
        prefix = at("prefix", o, [P, P]); o += 512
        chosen = at("chosen", o, [P, P]); o += 512
        code = at("code", o, [P, 1]); o += 32
        code_row = at("code_row", o, [1, 16], I32); o += 64
        n_over_i = at("n_over_i", o, [1, 1], I32); o += 32
        iota_i = at("iota_i", o, [P, P], I32)
        token_of = at("token_of", o, [P, P], I32); o += 512
        st2 = at("st2", o, [P, 6, TT]); o += 96
        assert o <= o_misc + 1408 + 1536 + 8 * KB, o - o_misc
        o = o_misc
        hot = at("hot", o, [2 * EXPERTS, P], F32R); o += 512
        tok_now = at("tok_now", o, [P, 1], I32); o += 32
        asg_now = at("asg_now", o, [P, 1], I32); o += 32
        gate_now = at("gate_now", o, [P, 1]); o += 32
        fence = at("fence", o, [P, 3]); o += 32
        assert o <= o_misc + 1408
        onehots = at("onehots", o_2 + 16 * KB, [P, TT, TOP_K, EXPERTS])
        picked = at("picked", o_2 + 18 * KB, [P, TT, TOP_K, EXPERTS])
        asg_of = at("asg_of", o_misc + 14080, [P, P], I32)
        gate_of = at("gate_of", o_misc + 14592, [P, P])
        hots = at("hots", o_2 + 24 * KB, [P, 4, 4, P])
        h2_rows = nc.dram_tensor("h2_rows", (T, D), F32).ap()
        y_rows = nc.dram_tensor("y_rows", (T * TOP_K, D), F32).ap()

        prow_full, x_full, consts = sem("prow_full"), sem("x_full"), sem("consts")
        ada1_full = [sem(f"ada1_full{i}") for i in range(KC)]
        acc1_step = sem("acc1_step")
        pcol_mm, pcol_done, sig_c, cact_done = sem("pcol_mm"), sem("pcol_done"), sem("sig_c"), sem("cact_done")
        ss_done, ms_done, sq_done, rs_done, xn_done = sem("ss_done"), sem("ms_done"), sem("sq_done"), sem("rs_done"), sem("xn_done")
        xT_mm, xT_done, mod_mm, mod_step = sem("xT_mm"), sem("xT_done"), sem("mod_mm"), sem("mod_step")
        h_f, h_hi, h_lo = sem("h_f"), sem("h_hi"), sem("h_lo")
        raw_full = [sem(f"raw_full{i}") for i in range(RING)]
        w_hi, w_lo = sem("w_hi"), sem("w_lo")
        mm_done = sem("mm_done")
        bank_read = sem("bank_read")
        sg_done, conv = sem("sg_done"), sem("conv")
        c_done, t3_step, s_f, s_hi, s_lo = sem("c_done"), sem("t3_step"), sem("s_f"), sem("s_hi"), sem("s_lo")
        pool_step = sem("pool_step")
        p_hi, p_lo, mg_step = sem("p_hi"), sem("p_lo"), sem("mg_step")
        mean_mm, mu_done, cen_done, sq2_done, var_mm, var_e, lsd_done, lrs_done = (
            sem("mean_mm"), sem("mu_done"), sem("cen_done"), sem("sq2_done"), sem("var_mm"), sem("var_e"), sem("lsd_done"), sem("lrs_done"))
        xh_done, z_done, vf_done, v_hi, v_lo = sem("xh_done"), sem("z_done"), sem("vf_done"), sem("v_hi"), sem("v_lo")
        m_hi, m_lo = sem("m_hi"), sem("m_lo")
        ada_full = [sem(f"ada_full{i}") for i in range(RING)]
        ada_used = sem("ada_used")
        row_mm, row_done = sem("row_mm"), sem("row_done")
        brow0_full, brow_full, gbc_full, x2_full, wr_full = (
            sem("brow0_full"), sem("brow_full"), sem("gbc_full"), sem("x2_full"), sem("wr_full"))
        g1_ready, x2_step, x2_done, y_mm, row_biased = sem("g1_ready"), sem("x2_step"), sem("x2_done"), sem("y_mm"), sem("row_biased")
        squared, mean_sq, inv_done, sd_done, mod2_done, b2_done, h2_step, h2_done = (
            sem("squared"), sem("mean_sq"), sem("inv_done"), sem("sd_done"), sem("mod2_done"), sem("b2_done"), sem("h2_step"), sem("h2_done"))
        h2_tr, h2T_done, logit_mm, h2_stored = sem("h2_tr"), sem("h2T_done"), sem("logit_mm"), sem("h2_stored")
        routed, negmax_done, exp_done = sem("routed"), sem("negmax_done"), sem("exp_done")
        mark_done, rank_mm, code_done, code_mm, codes_ready = (
            sem("mark_done"), sem("rank_mm"), sem("code_done"), sem("code_mm"), sem("codes_ready"))
        logit_read, router_mm, lT_done = sem("logit_read"), sem("router_mm"), sem("lT_done")
        consts2, hots_done, table_mm, tokens_ready = sem("consts2"), sem("hots_done"), sem("table_mm"), sem("tokens_ready")
        bst_full, bias_hi, bias_ready = sem("bst_full"), sem("bias_hi"), sem("bias_ready")
        craw_full = [sem(f"craw_full{p}") for p in range(RAW_RING // 2)]
        c_hi = sem("c_hi")
        c_lo = sem("c_lo")
        c_mm = sem("c_mm")
        xg_full, xe_tr, xe_hi, xe_lo = sem("xg_full"), sem("xe_tr"), sem("xe_hi"), sem("xe_lo")
        hot_ready, hot_used, gate_ready, asg_ready = sem("hot_ready"), sem("hot_used"), sem("gate_ready"), sem("asg_ready")
        tok_ready = sem("tok_ready")
        gt_done, clip_done, up_done, act_done, sgm_done = (
            sem("gt_done"), sem("clip_done"), sem("up_done"), sem("act_done"), sem("sgm_done"))
        ae_tr, ae_hi, ae_lo, yg_done, y_put = sem("ae_tr"), sem("ae_hi"), sem("ae_lo"), sem("yg_done"), sem("y_put")
        moe_done = sem("moe_done")
        scaled = sem("scaled")
        yt_full = ada1_full
        sum_step, sqz_done, stat3, sd3_done, out_step, out_ready, stored = (
            sem("sum_step"), sem("sqz_done"), sem("stat3"), sem("sd3_done"), sem("out_step"), sem("out_ready"), sem("stored"))

        def w_in_block(col, i):
            return w_in[0, :, ds(i * P + col, P)].rearrange("(k p) n -> p k n", p=P)

        def square_block(w, i):
            return w[0, :, ds(i * P, P)].rearrange("(k p) n -> p k n", p=P)

        raw_blk = [raw[:, s, :].rearrange("p (k n) -> p k n", k=KC) for s in range(RING)]

        block = ctx.enter_context(nc.Block())

        @block.sync
        def _(sp):
            sp.dma_start(x_in[:], x[0].rearrange("(t p) n -> p t n", p=P)).then_inc(x_full, 16)
            for r, src in ((R_C, cond), (R_MIXG, mix_pre_g), (R_CFB, cf_conv_b), (R_LNG, cf_ln_g), (R_LNB, cf_ln_b),
                           (R_CFOB, cf_out_b), (R_POOLS, pool_scale)):
                sp.dma_start(prow[r:r + 1, :], src[0:1, :]).then_inc(prow_full, 16)
            sp.dma_start(prow[R_SHIFT1:R_SHIFT1 + 2, :], ada_b[0, 0:2 * D].rearrange("(r n) -> r n", r=2)).then_inc(prow_full, 16)
            sp.dma_start(prow[R_SC:R_SC + SC_W, :], sc_conv[0]).then_inc(prow_full, 16)
            sp.dma_start(prow[R_CF:R_CF + CF_W, :], cf_conv[0]).then_inc(prow_full, 16)
            for k in range(KC):
                sp.dma_start(ada1[:, k, :], ada_w[0, k * P:(k + 1) * P, 0:2 * D]).then_inc(ada1_full[k], 16)

            def load(n, s, dst, src):
                if not isinstance(src.offset, int):
                    sp.lower_val(src.offset * 4)
                sp.wait_ge(w_lo, n + 1)
                sp.dma_start(dst, src).then_inc(raw_full[s], 16)

            def chunk_pair(e, c):
                k = c % 8
                if c < 16:
                    h = c // 8
                    return w_gu[0, ds(e, 1), k * P:(k + 2) * P, :].rearrange("e (p i) (u n) -> p (e i u) n", i=2, u=2)[:, :, h * HALF:(h + 1) * HALF]
                return w_down[0, ds(e, 1), k * P:(k + 2) * P, :].rearrange("e (p i) n -> p (e i n)", i=2)

            def pair_slots(c):
                dst = craw2[c // 2 % (RAW_RING // 2)]
                return dst[:, :, :].rearrange("p k (u n) -> p (k u) n", u=2) if c < 16 else dst[:, :, :].rearrange("p k n -> p (k n)")

            def first_pair(c):
                sp.dma_start(pair_slots(c), chunk_pair(0, c)).then_inc(craw_full[c // 2], 16)

            def next_pair(blk, e, c):
                src = chunk_pair(e, c)
                if not isinstance(src.offset, int):
                    sp.lower_val(src.offset * 4)
                last = (c + 1 - RAW_RING) % CH
                of = blk + 1 if c >= RAW_RING else blk
                if last in WHOLE:
                    sp.wait_ge(c_mm, of * CH + (last + 1))
                else:
                    sp.wait_ge(c_lo, of * NS + splits_before(last + 1))
                sp.dma_start(pair_slots(c), src).then_inc(craw_full[c // 2 % (RAW_RING // 2)], 16)

            with sp.Fori(0, 4) as j:
                for s in range(RING):
                    load(j * 4 + (N_A + s), s, raw_blk[s], w_in_block((3 + s % 2) * D, j * 2 + s // 2))
            with sp.Fori(0, 8) as i:
                for s, part in enumerate((1, 2, 0, 5)):
                    load(i * 4 + (N_B + s), s, raw_blk[s], w_in_block(part * D, i))
            sp.wait_ge(xT_mm, KC)
            sp.dma_start(brow0, ada_b[0:1, 2 * D:3 * D]).then_inc(brow0_full, 16)
            with sp.Fori(0, 4) as j:
                for s in range(RING):
                    i = j * 2 + s // 2
                    load(j * 4 + (N_C + s), s, raw_blk[s], w_in_block(6 * D, i) if s % 2 == 0 else square_block(sc_out, i))
            for g in range(POOLS):
                for s in range(RING):
                    h = s // 2
                    if s % 2 == 0:
                        load(N_D + 4 * g + s, s, raw_blk[s], w_in_block(8 * D, 2 * g + h))
                    else:
                        load(N_D + 4 * g + s, s, raw_blk[s][:, 0:2, :],
                             pool_w[0, g, :, h * P:(h + 1) * P].rearrange("(k p) n -> p k n", p=P))
            with sp.Fori(0, 2) as j:
                for s in range(RING):
                    load(j * 4 + (N_E + s), s, raw_blk[s], w_in_block(7 * D, j * 4 + s))
            with sp.Fori(0, 2) as j:
                for s in range(RING):
                    load(j * 4 + (N_G + s), s, raw_blk[s], square_block(cf_out, j * 4 + s))
            for k in range(KC):
                load(N_F + k, k % RING, raw[:, k % RING, :], w_o[0, k * P:(k + 1) * P, :])
                if k == 5:
                    sp.wait_ge(mm_done, N_F + RING)
                    sp.dma_start(brow[0:1, :, :], ada_b[0:1, 3 * D:6 * D].rearrange("a (r n) -> a r n", r=3)).then_inc(brow_full, 16)
            sp.wait_ge(mm_done, N_F + RING)
            sp.wait_ge(m_lo, KC)
            sp.dma_start(wr[:, :, :], w_router[0].rearrange("(k p) e -> p k e", p=P)).then_inc(wr_full, 16)
            sp.dma_start(brt[:, :], b_router[0:1, :].broadcast_to((P, EXPERTS))).then_inc(wr_full, 16)
            sp.wait_ge(ada_used, 4 * KC)
            for r, src in enumerate((mix_post_g, moe_pre_g, moe_post_g)):
                sp.dma_start(gbc[:, r, :], src[0:1, :].broadcast_to((P, D))).then_inc(gbc_full, 16)
            sp.dma_start(x2[:], x[0].rearrange("(t p) n -> p t n", p=P)).then_inc(x2_full, 16)
            for c in range(0, 8, 2):
                first_pair(c)
            sp.wait_ge(ada_used, 4 * KC + RING)
            for c in range(8, RAW_RING, 2):
                first_pair(c)
            sp.wait_ge(y_mm, TT)
            for a in range(2):
                rows_a = slice(a * EXPERTS, (a + 1) * EXPERTS)
                sp.dma_start(bst[rows_a, 0:2 * D], b_gu[0]).then_inc(bst_full, 16)
                sp.dma_start(bst[rows_a, 2 * D:3 * D], b_down[0]).then_inc(bst_full, 16)
            for t in range(TT):
                sp.wait_ge(h2_done, t + 1)
                sp.dma_start(h2_rows[t * P:(t + 1) * P, :], h2[:, t, :]).then_inc(h2_stored, 16)

            with sp.Fori(0, EXPERTS - 1) as j:
                for c in range(RAW_RING, CH, 2):
                    next_pair(j, j, c)
                for c in range(0, RAW_RING, 2):
                    next_pair(j + 1, j + 1, c)
            for c in range(RAW_RING, CH, 2):
                next_pair(EXPERTS - 1, EXPERTS - 1, c)
            sp.wait_ge(codes_ready, 2)
            n_over = sp.value_load(n_over_i[0:1, 0:1], min_val=0, max_val=MAX_OVER)
            with sp.Fori(0, MAX_OVER) as j:
                with sp.If(j < n_over):
                    code_j = sp.value_load(code_row[0:1, ds(j, 1)], min_val=0, max_val=P - 1)
                    for c in range(0, CH, 2):
                        next_pair(j + EXPERTS, code_j // 4, c)
            sp.wait_ge(moe_done, 1)
            for t in range(TT):
                of_tile = y_rows[t * P * TOP_K:(t + 1) * P * TOP_K, :].rearrange("(p k) n -> p k n", k=TOP_K)
                for h in range(2):
                    sp.dma_start(yt[:, t, 2 * h:2 * h + 2, :], of_tile[:, 2 * h:2 * h + 2, :]).then_inc(yt_full[2 * t + h], 16)
            for t in range(TT):
                sp.wait_ge(out_ready, t + 1)
                sp.dma_start(out[0, t * P:(t + 1) * P, :], x2[:, t, :]).then_inc(stored, 16)
            sp.wait_ge(stored, TT * 16)

        @block.scalar
        def _(act):
            act.wait_ge(x_full, 16)
            for t in range(TT):
                act.activation(tmp[:, :, :].rearrange("p a b -> p (a b)"), x_in[:, t, :], ACT.Square,
                               accum_out=ss[:, t:t + 1]).then_inc(ss_done, 1)
                act.wait_ge(ss_done, t + 1)
            act.wait_ge(ms_done, 1)
            act.activation(rr[:, :], rs[:, :], ACT.Sqrt).then_inc(sq_done, 1)
            act.wait_ge(pcol_mm, 1)
            act.activation(pcol[:, :, :], ps[:, 0, 0:KC * N_ROWS].rearrange("p (k r) -> p k r", k=KC), ACT.Copy).then_inc(pcol_done, 1)
            act.wait_ge(pcol_done, 1)
            act.activation(csig[:, :], pcol[:, :, R_C], ACT.Sigmoid).then_inc(sig_c, 1)
            for k in range(KC):
                act.wait_ge(xT_mm, k + 1)
                act.activation(xT[:, k, :], ps[:, 1 + k % 4, :], ACT.Copy).then_inc(xT_done, 1)

            def hi(n, s, cols=D):
                act.wait_ge(raw_full[s], (n // RING) * 16 + 16)
                act.wait_ge(mm_done, n + 1)
                act.activation(split[:, s, 0, 0:cols], raw[:, s, 0:cols], ACT.Copy).then_inc(w_hi, 1)

            def hi_at(j, n0, s, cols=D):
                act.wait_ge(raw_full[s], j * 16 + (n0 // RING * 16 + 16))
                act.wait_ge(mm_done, j * 4 + (n0 + 1))
                act.activation(split[:, s, 0, 0:cols], raw[:, s, 0:cols], ACT.Copy).then_inc(w_hi, 1)

            def sigmoid(b, par, n):
                act.wait_ge(bank_read, n + 2)
                act.activation(sg[:, par, :], ps[:, b, :], ACT.Sigmoid).then_inc(sg_done, 1)

            hi(0, 0)
            hi(1, 1)
            for k in range(KC):
                act.wait_ge(h_f, k + 1)
                act.activation(hT[:, 0, k, :], htmp[:, k, :], ACT.Copy).then_inc(h_hi, 1)
            with act.Fori(0, 4) as j:
                for q in range(2):
                    n = N_A + 2 * q
                    hi_at(j, n + 2, (n + 2) % RING)
                    hi_at(j, n + 3, (n + 3) % RING)
                    act.wait_ge(mm_done, j * 4 + (n + 2 + RING))
                    sigmoid(2 * q + 1, q, j * 4 + n)
            with act.Fori(0, 8) as i:
                n = N_B
                hi_at(i, n + 2, 2)
                hi_at(i, n + 3, 3)
                act.wait_ge(mm_done, i * 4 + (n + 1 + RING))
                act.wait_ge(bank_read, i * 4 + (n + RING))
                act.activation(c_sb[:, :], ps[:, 0, :], ACT.Copy).then_inc(c_done, 1)
                hi_at(i, n + 4, 0)
                hi_at(i, n + 5, 1)
                act.wait_ge(s_f, i + 1)
                act.activation(sT[:, 0, ds(i, 1), :].rearrange("p a n -> p (a n)"), t3[:, :], ACT.Copy).then_inc(s_hi, 1)
            with act.Fori(0, 4) as j:
                for q in range(2):
                    n = N_C + 2 * q
                    hi_at(j, n + 2, (n + 2) % RING)
                    hi_at(j, n + 3, (n + 3) % RING)
                    act.wait_ge(mm_done, j * 4 + (n + 1 + RING))
                    sigmoid(2 * q, q, j * 4 + n)
            for g in range(POOLS):
                n = N_D + 4 * g
                act.wait_ge(mm_done, n + RING)
                for h in range(2):
                    act.activation(pS[:, 0, h, :], pT[:, 2 * g + h, :], ACT.Copy).then_inc(p_hi, 1)
                hi(n + 2, 2)
                hi(n + 3, 3, 2 * P)
                for h in range(2):
                    act.wait_ge(mm_done, n + 2 * h + 1 + RING)
                    sigmoid(2 * h, h, n + 2 * h)
                    if h == 0:
                        hi(n + 4, 0)
                        hi(n + 5, 1, 2 * P if g < POOLS - 1 else D)

            def gate1(i):
                act.wait_ge(mm_done, N_E + i + 1 + RING)
                act.wait_ge(p_lo, KC)
                act.wait_ge(sg_done, 3 * KC)
                gate = sgp[:, i, :] if i < KC - 1 else sg[:, 0, :]
                act.activation(gate, ps[:, i % RING, :], ACT.Sigmoid).then_inc(bank_read, 1)

            def square(k):
                act.wait_ge(cen_done, k + 1)
                if k >= 2:
                    act.wait_ge(var_mm, k - 1)
                act.activation(sq[:, k % 2, :], cv[:, k, :], ACT.Square).then_inc(sq2_done, 1)

            def norm(k):
                act.wait_ge(xh_done, k + 1)
                if k >= 2:
                    act.wait_ge(vf_done, k - 1)
                act.activation(tmp[:, k % 2, :], cv[:, k, :], ACT.Sigmoid, bias=pcol[:, k, R_LNB:R_LNB + 1],
                               scale=pcol[:, k, R_LNG:R_LNG + 1]).then_inc(z_done, 1)
                act.activation(zl[:, k % 2, :], cv[:, k, :], ACT.Identity, bias=pcol[:, k, R_LNB:R_LNB + 1],
                               scale=pcol[:, k, R_LNG:R_LNG + 1]).then_inc(z_done, 1)

            def norm_hi(k):
                act.wait_ge(vf_done, k + 1)
                act.activation(vT[:, 0, k, :], cv[:, k, :], ACT.Copy).then_inc(v_hi, 1)

            def gate_hi(i):
                hi(N_E + i, i % RING)

            gate_hi(2)
            gate1(0)
            act.wait_ge(mean_mm, KC)
            act.activation(mu[:, :], ps[:, 4, :], ACT.Copy).then_inc(mu_done, 1)
            gate_hi(3)
            for k in range(KC):
                square(k)
            gate1(1)
            gate_hi(4)
            act.wait_ge(var_e, 1)
            act.activation(lrs[:, :], lrs[:, :], ACT.Sqrt).then_inc(lsd_done, 1)
            gate_hi(5)
            gate1(2)
            for i in range(4):
                norm(2 * i)
                if i >= 1:
                    norm_hi(2 * i - 1)
                norm(2 * i + 1)
                norm_hi(2 * i)
                gate_hi(6 + i)
                gate1(3 + i)
            norm_hi(KC - 1)
            gate1(KC - 1)
            for h in range(2):
                act.wait_ge(row_mm, h + 1)
                act.activation(rows[:, 0, h * HALF:(h + 1) * HALF], ps[:, 6 + h, :], ACT.Copy).then_inc(row_done, 1)
            for i in range(KC):
                hi(N_G + i + 2, (i + 2) % RING)
                act.wait_ge(mg_step, KC + i + 1)
                act.activation(mT[:, 0, i, :], merged[:, i, :], ACT.Copy).then_inc(m_hi, 1)
            for k in range(2, KC):
                hi(N_F + k, k % RING)
            def both(t):
                return ps[:, 2 * t:2 * t + 2, :].rearrange("p b n -> p (b n)")

            def square_y(t, before):
                act.wait_ge(y_mm, t + 1)
                act.wait_ge(squared, before)
                act.activation(scrap[:, :], both(t), ACT.Square, accum_out=st2[:, 0, t:t + 1]).then_inc(squared, 1)

            def square_x(t, before):
                act.wait_ge(x2_done, t + 1)
                act.wait_ge(squared, before)
                act.activation(scrap[:, :], x2[:, t, :], ACT.Square, accum_out=st2[:, 3, t:t + 1]).then_inc(squared, 1)

            def root(a, t, n):
                act.wait_ge(mean_sq, n)
                act.activation(st2[:, a + 2, t:t + 1], st2[:, a + 1, t:t + 1], ACT.Sqrt).then_inc(sd_done, 1)

            square_y(0, 0)
            root(0, 0, 1)
            square_y(1, 1)
            root(0, 1, 2)
            square_x(0, 2)
            root(3, 0, 3)
            square_y(2, 3)
            root(0, 2, 4)
            square_x(1, 4)
            root(3, 1, 5)
            square_y(3, 5)
            root(0, 3, 6)
            act.wait_ge(row_mm, 6)
            act.activation(rows[:, 1, :], both(1), ACT.Copy).then_inc(b2_done, 1)
            square_x(2, 6)
            root(3, 2, 7)
            square_x(3, 7)
            root(3, 3, 8)
            act.wait_ge(row_mm, 8)
            act.activation(rows[:, 3, :], both(2), ACT.Copy).then_inc(b2_done, 1)
            def copy_h2T(t):
                act.wait_ge(h2_tr, t + 1)
                if t >= 2:
                    act.wait_ge(router_mm, t - 1)
                b = 6 - t % 2 * 2
                act.activation(h2T[:, t % 2, :, :].rearrange("p k n -> p (k n)"), ps[:, b:b + 2, :].rearrange("p b n -> p (b n)"),
                               ACT.Copy).then_inc(h2T_done, 1)

            def copy_logits(t):
                act.wait_ge(router_mm, t + 1)
                if t >= 2:
                    act.wait_ge(logit_mm, t - 1)
                act.activation(lT[:, t % 2, :], ps[0:EXPERTS, 2 + t % 2, 0:P], ACT.Copy).then_inc(lT_done, 1)

            def bias_high(r):
                act.activation(bias[:, r * D:(r + 1) * D], bst[:, r * D:(r + 1) * D], ACT.Copy).then_inc(bias_hi, 1)

            def c_hi_part(blk, q):
                c = SPLITS[q]
                act.wait_ge(craw_full[c // 2 % (RAW_RING // 2)], blk * 32 + (c // RAW_RING * 16 + 16))
                if q >= SPLIT_RING:
                    act.wait_ge(c_mm, blk * CH + (CH + SPLITS[q - SPLIT_RING] + 1))
                else:
                    act.wait_ge(c_mm, blk * CH + (SPLITS[q - SPLIT_RING + NS] + 1))
                act.activation(csplit[:, q % SPLIT_RING, 0, :], craw[c % RAW_RING], ACT.Copy).then_inc(c_hi, 1)

            copy_h2T(0)
            copy_h2T(1)
            copy_logits(0)
            act.wait_ge(mod2_done, 2)
            c_hi_part(0, 0)
            copy_h2T(2)
            copy_logits(1)
            act.wait_ge(bst_full, 64)
            act.wait_ge(h2_done, TT)
            bias_high(0)
            c_hi_part(0, 1)
            copy_h2T(3)
            copy_logits(2)
            bias_high(1)
            c_hi_part(0, 2)
            copy_logits(3)
            bias_high(2)
            act.wait_ge(negmax_done, 1)
            for t in range(TT):
                act.activation(ex[:, t, :], top[:, t, 0:TOP_K], ACT.Exp, bias=negmax[:, t:t + 1],
                               accum_out=exsum[:, t:t + 1]).then_inc(exp_done, 1)
            for q in POOL_LO:
                c_hi_part(0, q)
            for a in range(TT * TOP_K):
                if a >= 4:
                    act.wait_ge(table_mm, a - 3)
                act.wait_ge(hots_done, 3 * a + 1)
                act.activation(hots[:, a % 4, 2, :], hots[:, a % 4, 3, :], ACT.Copy,
                               scale=gates[:, a // TOP_K, a % TOP_K:a % TOP_K + 1]).then_inc(scaled, 1)

            def xe_high(blk, h):
                act.wait_ge(xe_tr, blk * 2 + (h + 1))
                act.activation(xe[:, 0, 4 * h:4 * h + 4, :].rearrange("p k n -> p (k n)"), ps[:, 4 + h, :], ACT.Copy).then_inc(xe_hi, 1)
                if h == 1:
                    act.activation(xe_w[:, :, :].rearrange("p k n -> p (k n)"), ps[:, 5, 2 * P:4 * P], ACT.Copy).then_inc(xe_hi, 1)

            def sigmoid_gate(blk, h):
                act.wait_ge(gt_done, blk * 2 + (h + 1))
                act.wait_ge(act_done, blk * 2 + (h + 1))
                act.activation(sgm[:, :], gt[:, :], ACT.Sigmoid, scale=ALPHA).then_inc(sgm_done, 1)

            def ae_high(blk, h):
                act.wait_ge(ae_tr, blk * 2 + (h + 2))
                act.activation(ae[:, 0, 4 * h:4 * h + 4, :].rearrange("p k n -> p (k n)"), ps[:, 4 + h, :], ACT.Copy).then_inc(ae_hi, 1)
                act.activation(ae_w[:, h, :], ps[:, 4 + h, 3 * P:4 * P], ACT.Copy).then_inc(ae_hi, 1)

            def expert_begin(blk):
                for q in range(AHEAD):
                    c_hi_part(blk, q)
                for h in range(2):
                    xe_high(blk, h)

            def next_begin(nxt):
                xe_high(nxt, 0)
                for q in range(AHEAD):
                    c_hi_part(nxt, q)
                xe_high(nxt, 1)

            def expert(blk, nxt, done=AHEAD, over=None):
                for q in range(done, NS):
                    c_hi_part(blk, q)
                    c = SPLITS[q]
                    if c == P_CHAIN0:
                        sigmoid_gate(blk, 0)
                    if c == P_AE0:
                        ae_high(blk, 0)
                    if c == P_CHAIN1:
                        sigmoid_gate(blk, 1)
                    if c == P_AE1:
                        ae_high(blk, 1)
                if over is not None:
                    with act.If(over > 0):
                        next_begin(nxt)
                elif nxt is not None:
                    next_begin(nxt)
                act.wait_ge(c_mm, blk * CH + 2 * CH)
                act.wait_ge(gate_ready, blk + 1)
                act.wait_ge(asg_ready, blk + 1)
                act.activation(yg[:, :], ps[:, 6:8, :].rearrange("p b n -> p (b n)"), ACT.Copy,
                               scale=gate_now[:, 0:1]).then_inc(yg_done, 1)

            for q in range(POOL_LO.stop, 8):
                c_hi_part(0, q)
            for h in range(2):
                xe_high(0, h)
            act.wait_ge(bias_ready, 1)
            for q in range(8, SPLIT_RING):
                c_hi_part(0, q)
            expert(0, 1, done=SPLIT_RING)
            with act.Fori(1, EXPERTS - 1) as j:
                expert(j, j + 1)
            n_over = act.value_load(n_over_i[0:1, 0:1], min_val=0, max_val=MAX_OVER)
            expert(EXPERTS - 1, EXPERTS, over=n_over)
            with act.If(n_over > 0):
                expert(EXPERTS, None)
            with act.If(n_over > 1):
                with act.Fori(1, MAX_OVER) as j:
                    with act.If(j < n_over):
                        expert_begin(j + EXPERTS)
                        expert(j + EXPERTS, None)
            for t in range(TT):
                act.wait_ge(sum_step, 3 * t + 3)
                act.wait_ge(sqz_done, t)
                act.activation(scrap2[:, :], yt[:, t, 0, :], ACT.Square, accum_out=st2[:, 0, t:t + 1]).then_inc(sqz_done, 1)
                act.wait_ge(stat3, 2 * t + 1)
                act.activation(st2[:, 2, t:t + 1], st2[:, 1, t:t + 1], ACT.Sqrt).then_inc(sd3_done, 1)


        @block.vector
        def _(dve):
            dve.memset(v[:, :, 0:CF_PAD], 0.0).then_inc(w_lo, RING)
            dve.memset(ones[:, :], 1.0).then_inc(bank_read, RING)
            dve.memset(mean_w[:, :], 1.0 / D).then_inc(ada_used, RING)
            dve.engine_nop().then_inc(c_lo, NS)
            dve.engine_nop().then_inc(clip_done, 2)
            dve.engine_nop().then_inc(act_done, 1)
            dve.wait_ge(ss_done, TT)
            dve.tensor_scalar(rs[:, :], ss[:, :], 1.0 / D, NORM_EPS, ALU.mult, ALU.add).then_inc(ms_done, 1)
            dve.wait_ge(sq_done, 1)
            dve.reciprocal(rs[:, :], rr[:, :]).then_inc(rs_done, 1)
            dve.wait_ge(rs_done, 1)
            for t in range(TT):
                dve.tensor_scalar(x_in[:, t, :], x_in[:, t, :], rs[:, t:t + 1], None, ALU.mult).then_inc(xn_done, 1)
            dve.wait_ge(sig_c, 1)
            dve.tensor_tensor(cact[:, :], pcol[:, :, R_C], csig[:, :], ALU.mult).then_inc(cact_done, 1)
            for g in range(POOLS):
                dve.memset(invw[:, 2 * g:2 * g + 2], 1.0 / (2 << g)).then_inc(pool_step, 1)
            dve.wait_ge(consts, 4)
            for k in range(KC):
                win = 2 << (k // 2)
                dve.tensor_scalar(corr[:, k, :], pos[:, :], float(win), 1.0 / win, ALU.min, ALU.mult).then_inc(pool_step, 1)
            dve.wait_ge(pool_step, POOLS + KC)
            dve.reciprocal(corr[:, :, :], corr[:, :, :]).then_inc(pool_step, 1)
            POOL0 = POOLS + KC + 1

            def lo(n, s, cols=D):
                dve.wait_ge(w_hi, n + 1)
                dve.tensor_tensor(split[:, s, 1, 0:cols], raw[:, s, 0:cols], split[:, s, 0, 0:cols].bitcast(F32),
                                  ALU.subtract).then_inc(w_lo, 1)

            dve.wait_ge(cact_done, 1)
            for k in range(KC):
                dve.wait_ge(ada1_full[k], 16)
                if k == 0:
                    dve.tensor_scalar(acc1[:, :], ada1[:, k, :], cact[:, k:k + 1], None, ALU.mult).then_inc(acc1_step, 1)
                else:
                    dve.wait_ge(acc1_step, k)
                    dve.scalar_tensor_tensor(acc1[:, :], ada1[:, k, :], cact[:, k:k + 1], acc1[:, :], ALU.mult, ALU.add).then_inc(acc1_step, 1)
            lo(0, 0)
            lo(1, 1)
            dve.wait_ge(mod_mm, 1)
            dve.tensor_tensor(mod1[:, :, :], ps[:, 7, 0:2 * KC].rearrange("p (a k) -> p a k", a=2),
                              pcol[:, :, R_SHIFT1:R_SHIFT1 + 2].rearrange("p k a -> p a k"), ALU.add).then_inc(mod_step, 1)
            dve.wait_ge(mod_step, 1)
            dve.scalar_tensor_tensor(mod1[:, 1, :], mod1[:, 1, :], 1.0, pcol[:, :, R_MIXG], ALU.add, ALU.mult).then_inc(mod_step, 1)
            dve.wait_ge(mod_step, 2)
            dve.wait_ge(xT_done, KC)
            for k in range(KC):
                dve.tensor_scalar(htmp[:, k, :], xT[:, k, :], mod1[:, 1, k:k + 1], mod1[:, 0, k:k + 1], ALU.mult, ALU.add).then_inc(h_f, 1)
                if k >= 1:
                    dve.wait_ge(h_hi, k)
                    dve.tensor_tensor(hT[:, 1, k - 1, :], htmp[:, k - 1, :], hT[:, 0, k - 1, :].bitcast(F32), ALU.subtract).then_inc(h_lo, 1)
            dve.wait_ge(h_hi, KC)
            dve.tensor_tensor(hT[:, 1, KC - 1, :], htmp[:, KC - 1, :], hT[:, 0, KC - 1, :].bitcast(F32), ALU.subtract).then_inc(h_lo, 1)
            dve.wait_ge(h_lo, KC)
            dve.memset(cxp[:, 0:SC_W - 1], 0.0).then_inc(pool_step, 1)
            dve.memset(csp[:, 0:SUM_PAD], 0.0).then_inc(pool_step, 1)
            POOL0 = POOL0 + 2

            conv_steps = [0]

            def taps(i, phase):
                for tap in range(*TAPS[phase]):
                    src = v[:, i, tap:tap + T]
                    wt = pcol[:, i, R_CF + tap:R_CF + tap + 1]
                    if tap == 0:
                        dve.tensor_scalar(cv[:, i, :], src, wt, pcol[:, i, R_CFB:R_CFB + 1], ALU.mult, ALU.add).then_inc(conv, 1)
                    else:
                        dve.wait_ge(conv, conv_steps[0])
                        dve.scalar_tensor_tensor(cv[:, i, :], src, wt, cv[:, i, :], ALU.mult, ALU.add).then_inc(conv, 1)
                    conv_steps[0] += 1

            for i in range(KC):
                n = N_A + 2 * i
                b = n % RING
                lo(n + 2, (n + 2) % RING)
                lo(n + 3, (n + 3) % RING)
                dve.wait_ge(sg_done, i + 1)
                dve.tensor_tensor(v[:, i, CF_PAD:CF_PAD + T], ps[:, b, :], sg[:, i % 2, :], ALU.mult).then_inc(bank_read, 2)
                dve.wait_ge(bank_read, n + 2 + RING)
                taps(i, "A")
            for i in range(KC):
                n = N_B + 4 * i
                lo(n + 2, 2)
                lo(n + 3, 3)
                dve.wait_ge(c_done, i + 1)
                dve.wait_ge(mm_done, n + 2 + RING)
                dve.tensor_tensor(cxp[:, SC_W - 1:SC_W - 1 + T], ps[:, 1, :], c_sb[:, :], ALU.mult).then_inc(bank_read, 2)
                dve.wait_ge(bank_read, n + 2 + RING)
                dve.wait_ge(s_hi, i)
                dve.tensor_scalar(t3[:, :], cxp[:, 0:T], pcol[:, i, R_SC:R_SC + 1], None, ALU.mult).then_inc(t3_step, 1)
                for a in range(1, SC_W):
                    dve.wait_ge(t3_step, i * SC_W + a)
                    dve.scalar_tensor_tensor(t3[:, :], cxp[:, a:a + T], pcol[:, i, R_SC + a:R_SC + a + 1], t3[:, :],
                                             ALU.mult, ALU.add).then_inc(t3_step, 1)
                lo(n + 4, 0)
                lo(n + 5, 1)
                dve.wait_ge(t3_step, i * SC_W + SC_W)
                dve.wait_ge(mm_done, n + 3 + RING)
                dve.tensor_tensor(t3[:, :], t3[:, :], ps[:, 2, :], ALU.mult).then_inc(s_f, 1)
                taps(i, "B1")
                dve.wait_ge(mm_done, n + 4 + RING)
                dve.tensor_tensor_scan(csp[:, SUM_PAD:SUM_PAD + T], ps[:, 3, :], cxp[:, 0:T], 0.0, ALU.add, ALU.bypass).then_inc(pool_step, 1)
                dve.wait_ge(pool_step, i * 3 + (POOL0 + 1))
                win = 2 << (i // 2)
                dve.tensor_tensor(c_sb[:, :], csp[:, SUM_PAD:SUM_PAD + T], csp[:, SUM_PAD - win:SUM_PAD - win + T], ALU.subtract).then_inc(pool_step, 1)
                dve.wait_ge(pool_step, i * 3 + (POOL0 + 2))
                dve.tensor_tensor(c_sb[:, 0:MAX_WIN], c_sb[:, 0:MAX_WIN], corr[:, i, :], ALU.mult).then_inc(pool_step, 1)
                dve.wait_ge(pool_step, i * 3 + (POOL0 + 3))
                dve.scalar_tensor_tensor(pT[:, i, :], c_sb[:, :], invw[:, i:i + 1], ps[:, 3, :], ALU.mult, ALU.subtract).then_inc(bank_read, 2)
                dve.wait_ge(s_hi, i + 1)
                dve.tensor_tensor(sT[:, 1, i, :], t3[:, :], sT[:, 0, i, :].bitcast(F32), ALU.subtract).then_inc(s_lo, 1)
                taps(i, "B2")
            def pool_lo(g):
                for h in range(2):
                    dve.wait_ge(p_hi, 2 * g + h + 1)
                    dve.tensor_tensor(pS[:, 1, h, :], pT[:, 2 * g + h, :], pS[:, 0, h, :].bitcast(F32), ALU.subtract).then_inc(p_lo, 1)

            for i in range(KC):
                n = N_C + 2 * i
                b = n % RING
                lo(n + 2, (n + 2) % RING)
                lo(n + 3, (n + 3) % RING)
                dve.wait_ge(sg_done, i + KC + 1)
                dve.wait_ge(mm_done, n + 2 + RING)
                dve.tensor_tensor(merged[:, i, :], ps[:, b + 1, :], sg[:, i % 2, :], ALU.mult).then_inc(bank_read, 2)
                taps(i, "C1")
                if i == KC - 1:
                    pool_lo(0)
                    lo(N_D + 2, 2)
                    lo(N_D + 3, 3, 2 * P)
                taps(i, "C2")
            for g in range(POOLS):
                n = N_D + 4 * g
                if g >= 1:
                    pool_lo(g)
                    lo(n + 2, 2)
                    lo(n + 3, 3, 2 * P)
                for h in range(2):
                    m = 2 * g + h
                    dve.wait_ge(sg_done, 2 * KC + m + 1)
                    dve.wait_ge(mm_done, n + 2 * h + 2 + RING)
                    dve.wait_ge(mg_step, m)
                    dve.scalar_tensor_tensor(xtra[:, :], ps[:, 2 * h + 1, :], pcol[:, m, R_POOLS:R_POOLS + 1], sg[:, h, :],
                                             ALU.mult, ALU.mult).then_inc(bank_read, 2)
                    dve.wait_ge(bank_read, n + 2 * h + 2 + RING)
                    dve.tensor_tensor(merged[:, m, :], merged[:, m, :], xtra[:, :], ALU.add).then_inc(mg_step, 1)
                    if h == 0:
                        lo(n + 4, 0)
                        lo(n + 5, 1, 2 * P if g < POOLS - 1 else D)
                    taps(m, "D")

            def centre(k):
                dve.tensor_tensor(cv[:, k, :], cv[:, k, :], mu[:, :], ALU.subtract).then_inc(cen_done, 1)

            def silu(k):
                dve.wait_ge(z_done, 2 * k + 2)
                dve.tensor_tensor(cv[:, k, :], zl[:, k % 2, :], tmp[:, k % 2, :], ALU.mult).then_inc(vf_done, 1)

            def silu_lo(k):
                dve.wait_ge(v_hi, k + 1)
                dve.tensor_tensor(vT[:, 1, k, :], cv[:, k, :], vT[:, 0, k, :].bitcast(F32), ALU.subtract).then_inc(v_lo, 1)

            def ada_sum(q):
                r, k = q // KC, q % KC
                dve.wait_ge(ada_full[q % RING], (q // RING + 1) * 16)
                src = (ada_ring0 if r == 0 else ada_ring)[:, q % RING, :]
                if q == KC:
                    dve.wait_ge(row_biased, 1)
                if k == 0:
                    dve.tensor_scalar(rows[:, r, :], src, cact[:, k:k + 1], None, ALU.mult).then_inc(ada_used, 1)
                else:
                    dve.wait_ge(ada_used, q + RING)
                    dve.scalar_tensor_tensor(rows[:, r, :], src, cact[:, k:k + 1], rows[:, r, :],
                                             ALU.mult, ALU.add).then_inc(ada_used, 1)

            def gate_lo(i):
                lo(N_E + i, i % RING)

            gate_lo(2)
            dve.wait_ge(mu_done, 1)
            for k in range(KC):
                centre(k)
            gate_lo(3)
            for k in range(6):
                ada_sum(k)
            gate_lo(4)
            dve.wait_ge(var_mm, KC)
            dve.tensor_scalar(lrs[:, :], ps[:, 5, :], LN_EPS, None, ALU.add).then_inc(var_e, 1)
            ada_sum(6)
            ada_sum(7)
            dve.wait_ge(lsd_done, 1)
            dve.reciprocal(lrs[:, :], lrs[:, :]).then_inc(lrs_done, 1)
            gate_lo(5)
            dve.wait_ge(lrs_done, 1)
            dve.wait_ge(sq2_done, KC)
            for k in range(KC):
                dve.tensor_tensor(cv[:, k, :], cv[:, k, :], lrs[:, :], ALU.mult).then_inc(xh_done, 1)
                if k >= 1:
                    silu(k - 1)
                if k >= 2:
                    silu_lo(k - 2)
                if k % 2 == 1:
                    gate_lo(6 + k // 2)
            silu(KC - 1)
            silu_lo(KC - 2)
            silu_lo(KC - 1)
            dve.wait_ge(bank_read, N_G + RING)
            for i in range(KC):
                n = N_G + i
                lo(n + 2, (n + 2) % RING)
                dve.wait_ge(mm_done, n + 1 + RING)
                dve.wait_ge(mg_step, i + KC)
                gate = sgp[:, i, :] if i < KC - 1 else sg[:, 0, :]
                dve.scalar_tensor_tensor(xtra[:, :], ps[:, n % RING, :], pcol[:, i, R_CFOB:R_CFOB + 1], gate,
                                         ALU.add, ALU.mult).then_inc(bank_read, 1)
                dve.wait_ge(bank_read, n + 1 + RING)
                dve.tensor_tensor(merged[:, i, :], merged[:, i, :], xtra[:, :], ALU.add).then_inc(mg_step, 1)
                ada_sum(KC + i)
                dve.wait_ge(m_hi, i + 1)
                dve.tensor_tensor(mT[:, 1, i, :], merged[:, i, :], mT[:, 0, i, :].bitcast(F32), ALU.subtract).then_inc(m_lo, 1)
            for k in range(KC):
                if k >= 2:
                    lo(N_F + k, k % RING)
                for q in range(2):
                    ada_sum(2 * KC + 2 * k + q)
            dve.wait_ge(gbc_full, 48)
            dve.wait_ge(row_done, 2)
            dve.tensor_tensor(rows[:, 0, :], rows[:, 0, :], gbc[:, 0, :], ALU.mult).then_inc(g1_ready, 1)
            dve.wait_ge(g1_ready, 1)
            dve.wait_ge(x2_full, 16)

            def mean_square(a, t, n):
                dve.wait_ge(squared, n)
                dve.tensor_scalar(st2[:, a + 1, t:t + 1], st2[:, a, t:t + 1], 1.0 / D, NORM_EPS, ALU.mult, ALU.add).then_inc(mean_sq, 1)

            n_inv = [0]

            def invert(a, t, n):
                dve.wait_ge(sd_done, n)
                dve.reciprocal(st2[:, a, t:t + 1], st2[:, a + 2, t:t + 1]).then_inc(inv_done, 1)
                n_inv[0] += 1

            def residual(t):
                dve.wait_ge(inv_done, n_inv[0])
                dve.scalar_tensor_tensor(ynorm[:, :], both(t), st2[:, 0, t:t + 1], rows[:, 0, :], ALU.mult, ALU.mult).then_inc(x2_step, 1)
                dve.wait_ge(x2_step, t + 1)
                dve.tensor_tensor(x2[:, t, :], x2[:, t, :], ynorm[:, :], ALU.add).then_inc(x2_done, 1)
                dve.wait_ge(x2_done, t + 1)

            def both(t):
                return ps[:, 2 * t:2 * t + 2, :].rearrange("p b n -> p (b n)")

            mean_square(0, 0, 1)
            invert(0, 0, 1)
            mean_square(0, 1, 2)
            residual(0)
            invert(0, 1, 2)
            mean_square(3, 0, 3)
            residual(1)
            mean_square(0, 2, 4)
            invert(3, 0, 3)
            invert(0, 2, 4)
            residual(2)
            mean_square(3, 1, 5)
            invert(3, 1, 5)
            mean_square(0, 3, 6)
            dve.wait_ge(row_mm, 4)
            dve.scalar_tensor_tensor(rows[:, 2, :], both(0), 1.0, gbc[:, 1, :], ALU.add, ALU.mult).then_inc(mod2_done, 1)
            invert(0, 3, 6)
            residual(3)
            dve.wait_ge(mod2_done, 1)
            dve.wait_ge(b2_done, 1)
            for t in range(TT):
                if t >= 2:
                    mean_square(3, t, t + 5)
                    invert(3, t, t + 5)
                    dve.wait_ge(inv_done, t + 5)
                dve.scalar_tensor_tensor(h2[:, t, :], x2[:, t, :], st2[:, 3, t:t + 1], rows[:, 2, :], ALU.mult, ALU.mult).then_inc(h2_step, 1)
                dve.wait_ge(h2_step, t + 1)
                dve.tensor_tensor(h2[:, t, :], h2[:, t, :], rows[:, 1, :], ALU.add).then_inc(h2_done, 1)
            dve.wait_ge(b2_done, 2)
            dve.tensor_tensor(rows[:, 3, :], rows[:, 3, :], gbc[:, 2, :], ALU.mult).then_inc(mod2_done, 1)

            def c_lo_part(blk, q):
                c = SPLITS[q]
                dve.wait_ge(c_hi, blk * NS + (q + 1))
                dve.tensor_tensor(csplit[:, q % SPLIT_RING, 1, :], craw[c % RAW_RING],
                                  csplit[:, q % SPLIT_RING, 0, :].bitcast(F32), ALU.subtract).then_inc(c_lo, 1)

            n_r = [0]

            def step(ins):
                ins.then_inc(routed, 1)
                n_r[0] += 1
                dve.wait_ge(routed, n_r[0])

            dve.wait_ge(wr_full, 32)
            for t in range(TT):
                dve.wait_ge(logit_mm, t + 1)
                dve.tensor_tensor(logits[:, t, :], ps[:, t % 2, 0:EXPERTS], brt[:, :], ALU.add).then_inc(logit_read, 1)
                dve.wait_ge(logit_read, t + 1)
                step(dve.max(top[:, t, :], logits[:, t, :]))
                step(dve.max_index(topi[:, t, :], top[:, t, :], logits[:, t, :]))
                if t < TT - 1:
                    c_lo_part(0, t)
            dve.tensor_scalar(negmax[:, :], top[:, :, 0], -1.0, None, ALU.mult).then_inc(negmax_done, 1)
            step(dve.tensor_copy(idxf[:, :, :], topi[:, :, 0:TOP_K]))
            dve.memset(before[:, 0, :], 0.0)
            dve.wait_ge(consts2, 10)
            step(dve.tensor_tensor(onehots[:, :, :, :], iota_e[:, 0:EXPERTS].unsqueeze(1).unsqueeze(1).broadcast_to((P, TT, TOP_K, EXPERTS)),
                                   idxf[:, :, :].unsqueeze(3).broadcast_to((P, TT, TOP_K, EXPERTS)), ALU.is_equal))
            step(dve.tensor_reduce(mark[:, :, :], onehots[:, :, :, :].rearrange("p t k e -> p t e k"), AX.X, ALU.add))
            dve.tensor_copy(before[:, 1, :], mark[:, 0, :]).then_inc(mark_done, 1)
            for t in range(1, TT):
                dve.wait_ge(mark_done, t)
                dve.tensor_tensor(before[:, t + 1, :], before[:, t, :], mark[:, t, :], ALU.add).then_inc(mark_done, 1)
            dve.wait_ge(exp_done, TT)
            step(dve.reciprocal(exinv[:, :], exsum[:, :]))
            step(dve.tensor_tensor(gates[:, :, :], ex[:, :, :], exinv[:, :].unsqueeze(2).broadcast_to((P, TT, TOP_K)), ALU.mult))
            dve.wait_ge(rank_mm, 1)
            step(dve.tensor_tensor(picked[:, :, :, :], onehots[:, :, :, :],
                                   ps[:, 3, 0:P].rearrange("p (t e) -> p t e", t=TT).unsqueeze(2).broadcast_to((P, TT, TOP_K, EXPERTS)), ALU.mult))
            step(dve.tensor_reduce(rank[:, :, :], picked[:, :, :, :], AX.X, ALU.add))
            step(dve.tensor_scalar(beyond[:, :, :], rank[:, :, :], float(P), None, ALU.is_ge))
            for b in range(2, TOP_K):
                step(dve.scalar_tensor_tensor(beyond[:, :, :], rank[:, :, :], float(b * P), beyond[:, :, :], ALU.is_ge, ALU.add))
            step(dve.scalar_tensor_tensor(rank[:, :, :], beyond[:, :, :], float(-P), rank[:, :, :], ALU.mult, ALU.add))
            step(dve.scalar_tensor_tensor(column[:, :, :], idxf[:, :, :], 4.0, beyond[:, :, :], ALU.mult, ALU.add))
            for a in range(TT * TOP_K):
                t, k = a // TOP_K, a % TOP_K
                if a >= 4:
                    dve.wait_ge(table_mm, a - 3)
                m = a % 4
                dve.tensor_scalar(hots[:, m, 3, :], iota_e[:, :], column[:, t, k:k + 1], None, ALU.is_equal).then_inc(hots_done, 1)
                dve.tensor_scalar(hots[:, m, 0, :], iota_e[:, :], rank[:, t, k:k + 1], None, ALU.is_equal).then_inc(hots_done, 1)
                dve.tensor_scalar(hots[:, m, 1, :], iota_e[:, :], column[:, t, k:k + 1], number[:, a:a + 1], ALU.is_equal, ALU.mult).then_inc(hots_done, 1)
            dve.wait_ge(table_mm, TT * TOP_K)
            step(dve.tensor_scalar(asg_of[:, :], ps[:, 0, 0:P], float(NO_ROW), None, ALU.add))
            dve.tensor_scalar(token_of[:, :], asg_of[:, :], 2, None, ALU.arith_shift_right).then_inc(tokens_ready, 1)
            dve.tensor_copy(gate_of[:, :], ps[:, 0, P:2 * P]).then_inc(tokens_ready, 1)
            step(dve.memset(flags[:, :, 0], 0.0))
            for b in range(1, 4):
                step(dve.tensor_scalar(flags[:, :, b], ps[:, 3, P:P + EXPERTS], float(b * P) + 0.5, None, ALU.is_ge))
            flat = flags[:, :, :].rearrange("p e b -> p (e b)")
            step(dve.tensor_tensor_scan(prefix[:, :], flat, flat, 0.0, ALU.add, ALU.bypass))
            step(dve.scalar_tensor_tensor(chosen[:, :], prefix[:, :], pidx[:, 0:1], flat, ALU.is_equal, ALU.mult))
            step(dve.tensor_tensor(chosen[:, :], chosen[:, :], iota_e[:, :], ALU.mult))
            dve.tensor_reduce(code[:, :], chosen[:, :], AX.X, ALU.add).then_inc(code_done, 1)
            dve.tensor_copy(n_over_i[0:1, 0:1], prefix[0:1, P - 1:P]).then_inc(codes_ready, 1)
            dve.wait_ge(code_mm, 1)
            dve.tensor_copy(code_row[0:1, :], ps[0:1, 3, 2 * P:2 * P + 16]).then_inc(codes_ready, 1)
            def xe_low(blk, h):
                dve.wait_ge(xe_hi, blk * 3 + (2 * h + 1))
                dve.tensor_tensor(xe[:, 1, 4 * h:4 * h + 4, :].rearrange("p k n -> p (k n)"), ps[:, 4 + h, :],
                                  xe[:, 0, 4 * h:4 * h + 4, :].rearrange("p k n -> p (k n)").bitcast(F32), ALU.subtract).then_inc(xe_lo, 1)

            def ae_low(blk, h):
                dve.wait_ge(ae_hi, blk * 4 + (2 * h + 2))
                dve.tensor_tensor(ae[:, 1, 4 * h:4 * h + 4, :].rearrange("p k n -> p (k n)"), ps[:, 4 + h, :],
                                  ae[:, 0, 4 * h:4 * h + 4, :].rearrange("p k n -> p (k n)").bitcast(F32), ALU.subtract).then_inc(ae_lo, 1)

            def swiglu(blk, h):
                dve.wait_ge(c_mm, blk * CH + (CH + 8 * h + 8))
                dve.wait_ge(sgm_done, blk * 2 + (h + 1))
                dve.tensor_scalar(gt[:, :], ps[:, 2 * h, :], LIMIT, None, ALU.min).then_inc(gt_done, 1)
                dve.wait_ge(ae_tr, blk * 2 + (h + 1))
                dve.tensor_scalar(ua[:, :], ps[:, 2 * h + 1, :], -LIMIT, LIMIT, ALU.max, ALU.min).then_inc(clip_done, 1)
                dve.wait_ge(clip_done, blk * 2 + (h + 3))
                dve.scalar_tensor_tensor(ua[:, :], ua[:, :], 1.0, gt[:, :], ALU.add, ALU.mult).then_inc(up_done, 1)
                dve.wait_ge(up_done, blk * 2 + (h + 1))
                dve.wait_ge(sgm_done, blk * 2 + (h + 2))
                dve.tensor_tensor(ua[:, :], ua[:, :], sgm[:, :], ALU.mult).then_inc(act_done, 1)

            def expert_begin(blk):
                for q in range(AHEAD):
                    c_lo_part(blk, q)
                for h in range(2):
                    xe_low(blk, h)

            def next_begin(nxt):
                xe_low(nxt, 0)
                for q in range(AHEAD):
                    c_lo_part(nxt, q)
                xe_low(nxt, 1)

            def expert(blk, nxt, done=AHEAD, over=None):
                for q in range(done, NS):
                    c_lo_part(blk, q)
                    c = SPLITS[q]
                    if c == P_CHAIN0:
                        swiglu(blk, 0)
                    if c == P_AE0:
                        ae_low(blk, 0)
                    if c == P_CHAIN1:
                        swiglu(blk, 1)
                    if c == P_AE1:
                        ae_low(blk, 1)
                if over is not None:
                    with dve.If(over > 0):
                        next_begin(nxt)
                elif nxt is not None:
                    next_begin(nxt)

            dve.wait_ge(c_lo, NS + POOL_LO.stop)
            for q in range(POOL_LO.stop, 8):
                c_lo_part(0, q)
            for h in range(2):
                xe_low(0, h)
            for q in range(8, SPLIT_RING):
                c_lo_part(0, q)
            expert(0, 1, done=SPLIT_RING)
            with dve.Fori(1, EXPERTS - 1) as j:
                expert(j, j + 1)
            n_over = dve.value_load(n_over_i[0:1, 0:1], min_val=0, max_val=MAX_OVER)
            expert(EXPERTS - 1, EXPERTS, over=n_over)
            with dve.If(n_over > 0):
                expert(EXPERTS, None)
            with dve.If(n_over > 1):
                with dve.Fori(1, MAX_OVER) as j:
                    with dve.If(j < n_over):
                        expert_begin(j + EXPERTS)
                        expert(j + EXPERTS, None)
            def last_norm(t):
                dve.wait_ge(sqz_done, t + 1)
                dve.tensor_scalar(st2[:, 1, t:t + 1], st2[:, 0, t:t + 1], 1.0 / D, NORM_EPS, ALU.mult, ALU.add).then_inc(stat3, 1)
                dve.wait_ge(sd3_done, t + 1)
                dve.reciprocal(st2[:, 3, t:t + 1], st2[:, 2, t:t + 1]).then_inc(stat3, 1)
                dve.wait_ge(stat3, 2 * t + 2)
                dve.scalar_tensor_tensor(yt[:, t, 1, :], yt[:, t, 0, :], st2[:, 3, t:t + 1], rows[:, 3, :], ALU.mult, ALU.mult).then_inc(out_step, 1)
                dve.wait_ge(out_step, t + 1)
                dve.tensor_tensor(x2[:, t, :], x2[:, t, :], yt[:, t, 1, :], ALU.add).then_inc(out_ready, 1)

            for t in range(TT):
                for h in range(2):
                    dve.wait_ge(yt_full[2 * t + h], 32)
                    dve.tensor_tensor(yt[:, t, 2 * h, :], yt[:, t, 2 * h, :], yt[:, t, 2 * h + 1, :], ALU.add).then_inc(sum_step, 1)
                dve.wait_ge(sum_step, 3 * t + 2)
                dve.tensor_tensor(yt[:, t, 0, :], yt[:, t, 0, :], yt[:, t, 2, :], ALU.add).then_inc(sum_step, 1)
                if t >= 1:
                    last_norm(t - 1)
            last_norm(TT - 1)


        @block.gpsimd
        def _(pool):
            pool.engine_nop().then_inc(sgm_done, 1)
            pool.engine_nop().then_inc(yg_done, 1)

            def add_ada_b(r):
                pool.wait_ge(ada_used, (r + 1) * KC + RING)
                if r == 0:
                    pool.wait_ge(brow0_full, 16)
                else:
                    pool.wait_ge(brow_full, 16)
                    pool.wait_ge(row_biased, r)
                b_row = brow0 if r == 0 else brow[0:1, r - 1, :]
                pool.tensor_tensor(rows[0:1, r, :], rows[0:1, r, :], b_row, ALU.add).then_inc(row_biased, 1)

            def constants():
                pool.wait_ge(m_lo, KC)
                pool.iota(iota_i[:, :], pattern=[[1, P]], base=0, channel_multiplier=0).then_inc(consts2, 1)
                pool.iota(pidx_i[:, :], pattern=[[0, 1]], base=1, channel_multiplier=1).then_inc(consts2, 1)
                pool.iota(number_i[:, :, :], pattern=[[P * TOP_K, TT], [1, TOP_K]], base=-NO_ROW, channel_multiplier=TOP_K).then_inc(consts2, 1)
                pool.wait_ge(consts2, 3)
                pool.tensor_copy(iota_e[:, :], iota_i[:, :]).then_inc(consts2, 1)
                pool.tensor_copy(pidx[:, :], pidx_i[:, :]).then_inc(consts2, 1)
                pool.tensor_copy(number[:, :], number_i[:, :, :].rearrange("p t k -> p (t k)")).then_inc(consts2, 1)
                pool.affine_select(out=tri[:, :], in_=ones[:, :], compare_op=ALU.is_gt, fill=0.0, base=0,
                                   pattern=[[1, P]], channel_multiplier=-1).then_inc(consts2, 1)
                pool.wait_ge(consts2, 7)
                pool.tensor_copy(eye2[0:EXPERTS, :], ident[0:EXPERTS, 0:EXPERTS]).then_inc(consts2, 1)
                pool.wait_ge(consts2, 8)
                pool.tensor_copy(eye2[EXPERTS:2 * EXPERTS, :], ident[EXPERTS:2 * EXPERTS, EXPERTS:2 * EXPERTS]).then_inc(consts2, 1)
                pool.wait_ge(consts2, 9)
                pool.memset(fence[:, :], 0.0).then_inc(consts2, 1)
                pool.wait_ge(consts2, 10)

            pool.memset(ident[:, :], 0.0).then_inc(consts, 1)
            pool.wait_ge(consts, 1)
            pool.affine_select(out=ident[:, :], in_=ident[:, :], compare_op=ALU.not_equal, fill=1.0, base=0,
                               pattern=[[-1, P]], channel_multiplier=1).then_inc(consts, 1)
            pool.iota(pos_i[:, :], pattern=[[1, MAX_WIN]], base=1, channel_multiplier=0).then_inc(consts, 1)
            pool.wait_ge(consts, 3)
            pool.tensor_copy(pos[:, :], pos_i[:, :]).then_inc(consts, 1)
            pool.wait_ge(mm_done, N_D + RING)
            for k in range(KC):
                pool.wait_ge(ada_used, k + 1)
                pool.dma_start(ada_ring0[:, k % RING, :], ada_w[0, k * P:(k + 1) * P, 2 * D:3 * D]).then_inc(ada_full[k % RING], 16)
            add_ada_b(0)
            pool.wait_ge(v_lo, KC)
            for r in range(1, 4):
                for k in range(KC):
                    pool.wait_ge(ada_used, r * KC + k + 1)
                    pool.dma_start(ada_ring[:, k % RING, :], ada_w[0, k * P:(k + 1) * P, (r + 2) * D:(r + 3) * D]).then_inc(ada_full[k % RING], 16)
                    if r == 3 and k == RING - 1:
                        add_ada_b(1)
            add_ada_b(2)
            constants()
            add_ada_b(3)
            pool.wait_ge(h2_stored, TT * 16)
            pool.wait_ge(h2_tr, TT)
            pool.wait_ge(row_biased, 4)
            pool.memset(xg[:, :], 0.0).then_inc(consts2, 1)
            pool.wait_ge(consts2, 11)
            last_token, last_row = pool.to_reg(T - 1), pool.to_reg(T * TOP_K - 1)

            def gather(blk, col):
                pool.wait_ge(xg_full, blk * 16)
                pool.tensor_copy(tok_now[:, :], token_of[:, ds(col, 1)]).then_inc(tok_ready, 1)
                pool.wait_ge(tok_ready, blk + 1)
                pool.wait_ge(xe_tr, blk * 2)
                pool.tensor_tensor(fence[:, 0:1], fence[:, 1:2], fence[:, 1:2], ALU.add)
                pool.indirect_dma_start(out=xg[:, :], out_offset=None, in_=h2_rows,
                                        in_offset=bass.IndirectOffsetOnAxis(ap=tok_now[:, 0:1], axis=0),
                                        bounds_check=last_token, oob_is_err=False).then_inc(xg_full, 16)

            def choose(blk, e):
                pool.wait_ge(hot_used, blk)
                pool.tensor_copy(hot[:, :], eye2[:, ds(e, 1)].broadcast_to((2 * EXPERTS, P))).then_inc(hot_ready, 1)

            def labels(blk, col):
                pool.wait_ge(yg_done, blk + 1)
                pool.tensor_copy(gate_now[:, :], gate_of[:, ds(col, 1)]).then_inc(gate_ready, 1)
                pool.wait_ge(y_put, blk * 16)
                pool.tensor_copy(asg_now[:, :], asg_of[:, ds(col, 1)]).then_inc(asg_ready, 1)

            def scatter(blk):
                pool.wait_ge(yg_done, blk + 2)
                pool.wait_ge(asg_ready, blk + 1)
                pool.tensor_tensor(fence[:, 2:3], fence[:, 1:2], fence[:, 1:2], ALU.add)
                pool.indirect_dma_start(out=y_rows, out_offset=bass.IndirectOffsetOnAxis(ap=asg_now[:, 0:1], axis=0),
                                        in_=yg[:, :], in_offset=None,
                                        bounds_check=last_row, oob_is_err=False).then_inc(y_put, 16)

            pool.wait_ge(bias_hi, 3)
            pool.tensor_tensor(bias[EXPERTS:2 * EXPERTS, :], bst[EXPERTS:2 * EXPERTS, :], bias[EXPERTS:2 * EXPERTS, :].bitcast(F32),
                               ALU.subtract).then_inc(bias_ready, 1)
            pool.wait_ge(bias_ready, 1)
            for q in POOL_LO:
                pool.wait_ge(c_hi, q + 1)
                pool.wait_ge(c_lo, NS + q)
                pool.tensor_tensor(csplit[:, q, 1, :], craw[SPLITS[q]], csplit[:, q, 0, :].bitcast(F32), ALU.subtract).then_inc(c_lo, 1)
            pool.wait_ge(c_lo, NS + POOL_LO.stop)
            pool.wait_ge(tokens_ready, 2)
            gather(0, 0)
            choose(0, 0)
            labels(0, 0)
            with pool.Fori(0, EXPERTS - 1) as j:
                gather(j + 1, j * 4 + 4)
                choose(j + 1, j + 1)
                scatter(j)
                labels(j + 1, j * 4 + 4)
            pool.wait_ge(codes_ready, 2)
            n_over = pool.value_load(n_over_i[0:1, 0:1], min_val=0, max_val=MAX_OVER)
            with pool.If(n_over > 0):
                code_0 = pool.value_load(code_row[0:1, 0:1], min_val=0, max_val=P - 1)
                gather(EXPERTS, code_0)
                choose(EXPERTS, code_0 // 4)
            scatter(EXPERTS - 1)
            with pool.If(n_over > 0):
                code_0 = pool.value_load(code_row[0:1, 0:1], min_val=0, max_val=P - 1)
                labels(EXPERTS, code_0)
                scatter(EXPERTS)
                pool.wait_ge(y_put, (EXPERTS + 1) * 16)
            with pool.If(n_over > 1):
                with pool.Fori(1, MAX_OVER) as j:
                    with pool.If(j < n_over):
                        code_j = pool.value_load(code_row[0:1, ds(j, 1)], min_val=0, max_val=P - 1)
                        gather(j + EXPERTS, code_j)
                        choose(j + EXPERTS, code_j // 4)
                        labels(j + EXPERTS, code_j)
                        scatter(j + EXPERTS)
                        pool.wait_ge(y_put, j * 16 + (EXPERTS + 1) * 16)
            pool.wait_ge(y_put, EXPERTS * 16)
            pool.engine_nop().then_inc(moe_done, 1)


        @block.tensor
        def _(pe):
            pe.wait_ge(consts, 2)
            pe.matmul(ps[:, 6, 0:1], ident[:, :], ident[:, 0:1], start=True, stop=True).then_inc(mm_done, RING)
            pe.matmul(ps[:, 6, 1:2], ident[:, :], ident[:, 0:1], start=True, stop=True).then_inc(c_mm, CH)
            pe.matmul(ps[:, 6, 2:3], ident[:, :], ident[:, 0:1], start=True, stop=True).then_inc(ae_tr, 1)
            pe.wait_ge(prow_full, 160)
            for k in range(KC):
                last = pe.transpose(ps[:, 0, k * N_ROWS:(k + 1) * N_ROWS], prow[0:N_ROWS, k * P:(k + 1) * P], ident[0:N_ROWS, 0:N_ROWS])
            last.then_inc(pcol_mm, 1)
            pe.wait_ge(xn_done, TT)
            for k in range(KC):
                if k >= 4:
                    pe.wait_ge(xT_done, k - 3)
                for t in range(TT):
                    last = pe.transpose(ps[:, 1 + k % 4, t * P:(t + 1) * P], x_in[:, t, k * P:(k + 1) * P], ident[:, :])
                last.then_inc(xT_mm, 1)
            pe.wait_ge(acc1_step, KC)
            for m in range(2 * KC):
                last = pe.matmul(ps[:, 7, m:m + 1], acc1[:, m * P:(m + 1) * P], ones[:, 0:1], start=True, stop=True)
            last.then_inc(mod_mm, 1)

            def block(n, s, moving, ks=range(KC), arrives=None):
                pe.wait_ge(w_lo, n + (1 + RING))
                pe.wait_ge(bank_read, n + 1)
                for kk, k in enumerate(ks):
                    if arrives is not None:
                        pe.wait_ge(arrives, k + 1)
                    w_hi_k = split[:, s, 0, kk * P:(kk + 1) * P]
                    w_lo_k = split[:, s, 1, kk * P:(kk + 1) * P]
                    pe.matmul(ps[:, s, :], w_hi_k, moving[:, 0, k, :], start=(kk == 0), stop=False)
                    pe.matmul(ps[:, s, :], w_hi_k, moving[:, 1, k, :], start=False, stop=False)
                    last = pe.matmul(ps[:, s, :], w_lo_k, moving[:, 0, k, :], start=False, stop=(kk == len(ks) - 1))
                last.then_inc(mm_done, 1)

            for s in range(RING):
                block(N_A + s, s, hT, arrives=h_lo if s == 0 else None)
            with pe.Fori(1, 4) as j:
                for s in range(RING):
                    block(j * 4 + (N_A + s), s, hT)
            with pe.Fori(0, 8) as i:
                for s in range(RING):
                    block(i * 4 + (N_B + s), s, hT)
            with pe.Fori(0, 4) as j:
                for s in range(RING):
                    if s == 1:
                        pe.wait_ge(s_lo, KC)
                    block(j * 4 + (N_C + s), s, hT if s % 2 == 0 else sT)
            def mean_of(k):
                pe.wait_ge(conv, KC * TAPS["D"][0] + (k + 1) * (CF_W - TAPS["D"][0]))
                pe.matmul(ps[:, 4, :], mean_w[:, :], cv[:, k, :], start=(k == 0), stop=(k == KC - 1)).then_inc(mean_mm, 1)

            for g in range(POOLS):
                for s in range(RING):
                    if s == 1:
                        pe.wait_ge(p_lo, 2 * g + 2)
                    if s % 2 == 0:
                        block(N_D + 4 * g + s, s, hT)
                    else:
                        block(N_D + 4 * g + s, s, pS, range(2))
                if g >= 1:
                    mean_of(2 * g - 2)
                    mean_of(2 * g - 1)

            def gate_block(i):
                block(N_E + i, i % RING, hT)

            gate_block(0)
            mean_of(KC - 2)
            mean_of(KC - 1)
            gate_block(1)
            for k in range(KC):
                pe.wait_ge(sq2_done, k + 1)
                pe.matmul(ps[:, 5, :], mean_w[:, :], sq[:, k % 2, :], start=(k == 0), stop=(k == KC - 1)).then_inc(var_mm, 1)
            for i in range(2, KC):
                gate_block(i)

            def row_sum(r, b):
                for h in range(2):
                    pe.matmul(ps[:, b + h, :], ones[:, :], rows[:, r, h * HALF:(h + 1) * HALF], start=True, stop=True).then_inc(row_mm, 1)

            pe.wait_ge(row_biased, 1)
            row_sum(0, 6)
            for s in range(RING):
                block(N_G + s, s, vT, arrives=v_lo if s == 0 else None)
            for s in range(RING):
                block(N_G + RING + s, s, vT)

            pe.wait_ge(bank_read, N_F + RING)
            for ks in ((0,), (1,), (2,), (3,), (4,), (5,), (6, 7)):
                pe.wait_ge(w_lo, N_F + ks[-1] + 1 + RING)
                pe.wait_ge(m_lo, ks[-1] + 1)
                for t, k in ((t, k) for t in range(TT) for k in ks):
                    s = k % RING
                    if k == 0 and t == 3:
                        pe.wait_ge(row_done, 2)
                    for h in range(2):
                        o_ = ps[:, 2 * t + h, :]
                        w_h, w_l = (split[:, s, a, h * HALF:(h + 1) * HALF] for a in range(2))
                        m_h, m_l = (mT[:, a, k, t * P:(t + 1) * P] for a in range(2))
                        pe.matmul(o_, m_h, w_h, start=(k == 0), stop=False)
                        pe.matmul(o_, m_h, w_l, start=False, stop=False)
                        last = pe.matmul(o_, m_l, w_h, start=False, stop=(k == KC - 1))
                    if k == KC - 1:
                        last.then_inc(y_mm, 1)
                if len(ks) == 1:
                    last.then_inc(mm_done, 1)
            def turn_h2(t):
                b = 6 - t % 2 * 2
                pe.wait_ge(h2_done, t + 1)
                if t == 1:
                    pe.wait_ge(b2_done, 2)
                if t >= 2:
                    pe.wait_ge(h2T_done, t - 1)
                for k in range(KC):
                    last = pe.transpose(ps[:, b + k // 4, k % 4 * P:(k % 4 + 1) * P], h2[:, t, k * P:(k + 1) * P], ident[:, :])
                last.then_inc(h2_tr, 1)

            def router(t):
                pe.wait_ge(h2T_done, t + 1)
                if t >= 2:
                    pe.wait_ge(lT_done, t - 1)
                for k in range(KC):
                    last = pe.matmul(ps[0:EXPERTS, 2 + t % 2, 0:P], wr[:, k, :], h2T[:, t % 2, k, :], start=(k == 0), stop=(k == KC - 1))
                last.then_inc(router_mm, 1)

            def turn_logits(t):
                pe.wait_ge(lT_done, t + 1)
                if t >= 2:
                    pe.wait_ge(logit_read, t - 1)
                pe.transpose(ps[:, t % 2, 0:EXPERTS], lT[:, t % 2, :], ident[0:EXPERTS, 0:EXPERTS]).then_inc(logit_mm, 1)

            for n, r in enumerate((2, 1, 3)):
                pe.wait_ge(row_biased, r + 1)
                pe.wait_ge(x2_done, n + 1)
                row_sum(r, 2 * n)
            pe.wait_ge(wr_full, 32)
            pe.wait_ge(b2_done, 1)
            pe.wait_ge(mod2_done, 1)
            turn_h2(0)
            turn_h2(1)
            router(0)
            for t in range(2, TT):
                turn_h2(t)
                turn_logits(t - 2)
                router(t - 1)
            turn_logits(TT - 2)
            router(TT - 1)
            turn_logits(TT - 1)
            pe.wait_ge(mark_done, TT)
            pe.matmul(ps[:, 3, 0:P + EXPERTS], ones[:, :], before[:, :, :].rearrange("p t e -> p (t e)"), start=True, stop=False)
            pe.matmul(ps[:, 3, 0:P], tri[:, :], mark[:, :, :].rearrange("p t e -> p (t e)"), start=False, stop=True).then_inc(rank_mm, 1)
            for a in range(TT * TOP_K):
                pe.wait_ge(hots_done, 3 * a + 3)
                pe.wait_ge(scaled, a + 1)
                pe.matmul(ps[:, 0, 0:2 * P], hots[:, a % 4, 0, :], hots[:, a % 4, 1:3, :].rearrange("p b n -> p (b n)"),
                          start=(a == 0), stop=(a == TT * TOP_K - 1)).then_inc(table_mm, 1)
            pe.wait_ge(code_done, 1)
            pe.matmul(ps[0:1, 3, 2 * P:3 * P], code[:, 0:1], ident[:, :], start=True, stop=True).then_inc(code_mm, 1)

            def rows_of(k):
                first = k // 2 * 2 * P + k % 2
                return slice(first, first + 2 * P - 1, 2)

            def chunk(blk, c):
                if c < 16:
                    stand, stand_w, k, b = xe, xe_w[:, c % 2, :], c % 8, c // 8 * 2
                else:
                    stand, stand_w, k, b = ae, ae_w[:, (c - 16) // 4, :], c - 16, 6
                end = k == 7
                if c in WHOLE:
                    pe.wait_ge(craw_full[c // 2 % (RAW_RING // 2)], blk * 32 + (c // RAW_RING * 16 + 16))
                    for u in range(2):
                        last = pe.matmul(ps[:, b + u, :], stand_w, craw[c % RAW_RING][:, u * HALF:(u + 1) * HALF], start=False, stop=end)
                else:
                    q = SPLITS.index(c)
                    s = q % SPLIT_RING
                    pe.wait_ge(c_lo, blk * NS + (NS + q + 1))
                    for a, parts in ((0, (0, 1)), (1, (0,))):
                        for u in range(2):
                            for w in parts:
                                last = pe.matmul(ps[:, b + u, :], stand[:, a, k, :], csplit[:, s, w, u * HALF:(u + 1) * HALF],
                                                 start=False, stop=(end and a == 1))
                last.then_inc(c_mm, 1)

            def biases(banks, cols):
                for b, col in zip(banks, cols):
                    last = pe.matmul(ps[:, b, :], hot[:, :], bias[:, col:col + HALF], start=True, stop=False)
                return last

            def turn_tokens(blk, h):
                if h == 0:
                    pe.wait_ge(xg_full, blk * 16 + 16)
                for i in range(4):
                    k = 4 * h + i
                    last = pe.transpose(ps[:, 4 + h, i * P:(i + 1) * P], xg[:, rows_of(k)], ident[:, :])
                last.then_inc(xe_tr, 1)

            def turn_acts(blk, h):
                pe.wait_ge(act_done, blk * 2 + (h + 2))
                for i in range(4):
                    last = pe.transpose(ps[:, 4 + h, i * P:(i + 1) * P], ua[:, rows_of(i)], ident[:, :])
                last.then_inc(ae_tr, 1)

            def turn_next(nxt, over, h):
                if over is not None:
                    with pe.If(over > 0):
                        turn_tokens(nxt, h)
                elif nxt is not None:
                    turn_tokens(nxt, h)

            def expert(blk, nxt, over=None):
                pe.wait_ge(hot_ready, blk + 1)
                pe.wait_ge(clip_done, blk * 2 + 1)
                biases((0, 1), (0, D))
                pe.wait_ge(xe_lo, blk * 2 + 1)
                for c in range(4):
                    chunk(blk, c)
                pe.wait_ge(xe_lo, blk * 2 + 2)
                pe.wait_ge(xe_hi, blk * 3 + 3)
                for c in range(4, 8):
                    chunk(blk, c)
                pe.wait_ge(clip_done, blk * 2 + 2)
                biases((2, 3), (HALF, D + HALF))
                for c in range(8, 12):
                    chunk(blk, c)
                turn_acts(blk, 0)
                for c in range(12, 16):
                    chunk(blk, c)
                pe.wait_ge(yg_done, blk + 1)
                biases((6, 7), (2 * D, 2 * D + HALF)).then_inc(hot_used, 1)
                pe.wait_ge(ae_lo, blk * 2 + 1)
                pe.wait_ge(ae_hi, blk * 4 + 2)
                for c in range(16, 19):
                    chunk(blk, c)
                turn_acts(blk, 1)
                chunk(blk, 19)
                turn_next(nxt, over, 0)
                pe.wait_ge(ae_lo, blk * 2 + 2)
                pe.wait_ge(ae_hi, blk * 4 + 4)
                for c in range(20, 24):
                    chunk(blk, c)
                turn_next(nxt, over, 1)

            for h in range(2):
                turn_tokens(0, h)
            pe.wait_ge(bias_ready, 1)
            with pe.Fori(0, EXPERTS - 1) as j:
                expert(j, j + 1)
            n_over = pe.value_load(n_over_i[0:1, 0:1], min_val=0, max_val=MAX_OVER)
            expert(EXPERTS - 1, EXPERTS, over=n_over)
            with pe.If(n_over > 0):
                expert(EXPERTS, None)
            with pe.If(n_over > 1):
                with pe.Fori(1, MAX_OVER) as j:
                    with pe.If(j < n_over):
                        for h in range(2):
                            turn_tokens(j + EXPERTS, h)
                        expert(j + EXPERTS, None)


_INS = ["x", "c", "ada_w", "ada_b", "mix_pre_g", "mix_post_g", "w_in", "sc_conv", "sc_out", "cf_conv", "cf_conv_b",
        "cf_ln_g", "cf_ln_b", "cf_out", "cf_out_b", "pool_w", "pool_scale", "w_o", "moe_pre_g", "moe_post_g",
        "w_router", "b_router", "w_gu", "b_gu", "w_down", "b_down"]
_OUTS = [((1, 512, 1024), "float32")]


def kernel(**inputs):
    import numpy as _np
    import concourse.bacc as _bacc
    from concourse import mybir as _mybir
    from concourse.bass_utils import run_bass_kernel_spmd as _run

    nc = _bacc.Bacc("TRN2", target_bir_lowering=False, num_devices=1)
    arrays, args = {}, []
    for name in _INS:
        a = _np.ascontiguousarray(inputs[name])
        arrays[f"in_{name}_dram"] = a
        args.append(nc.dram_tensor(f"in_{name}_dram", a.shape, _mybir.dt.from_np(a.dtype), kind="ExternalInput").ap())
    for i, (shape, dtype) in enumerate(_OUTS):
        dt = _mybir.dt.from_np(_np.dtype(dtype))
        args.append(nc.dram_tensor(f"out_{i}_dram", shape, dt, kind="ExternalOutput").ap())
    build(nc, *args)
    r = _run(nc, [arrays], core_ids=[0])
    got = tuple(r.results[0][f"out_{i}_dram"] for i in range(len(_OUTS)))
    return got[0]
```
